# Optimizing a Trainium2 kernel written in Bass

```python
import math
import jax, jax.numpy as jnp
from jax import lax
import numpy as np

D_MODEL = 1024
BATCH = 1
SEQ = 512
DEPTH = 1
DEC_BATCH = 8
DEC_SEQ = 8
PAST_LEN = 1024
PAGE_SIZE = 128

HEAD_DIM = 64
ATTN_HEADS = 8
DILATED_GROUPS = ((128, 1), (512, 4), (2048, 16))
N_GROUPS = 3
ATTN_WIDTH = ATTN_HEADS * HEAD_DIM
RWKV_HEADS = 8
RWKV_WIDTH = RWKV_HEADS * HEAD_DIM
DECAY_LORA = 64
ICLR_LORA = 64
GATE_LORA = 128
D_FF = 2816
Q_BLOCK = 128
RMS_EPS = 1e-6
LN_X_EPS = 64e-5
ATTN_COLS = N_GROUPS * 3 * ATTN_WIDTH
SHIFT_SPLITS = (RWKV_WIDTH, 2 * RWKV_WIDTH, 3 * RWKV_WIDTH, 3 * RWKV_WIDTH + DECAY_LORA, 3 * RWKV_WIDTH + DECAY_LORA + ICLR_LORA)
SHIFT_COLS = 3 * RWKV_WIDTH + DECAY_LORA + ICLR_LORA + GATE_LORA
GATE_COLS = 2 * D_MODEL
IN_COLS = ATTN_COLS + SHIFT_COLS + GATE_COLS

kernel_name = 'hybrid_dilated_rwkv7_decoder_step'

def rmsnorm(x, g):
    xf = x.astype(jnp.float32)
    y = xf * lax.rsqrt(jnp.mean(xf * xf, axis=-1, keepdims=True) + RMS_EPS)
    return (y * g.astype(jnp.float32)).astype(x.dtype)

def half_swiglu(x, g, w_gate, w_up, w_down):
    h = rmsnorm(x, g)
    return x + 0.5 * ((jax.nn.silu(h @ w_gate) * (h @ w_up)) @ w_down)

def alibi_slopes(n_heads):
    return 2.0 ** (-8.0 * jnp.arange(1, n_heads + 1, dtype=jnp.float32) / n_heads)

def dilated_attn_prompt(q, k, v, window, dil):
    B, S, H, dh = q.shape
    n = S // dil
    nb = -(-n // Q_BLOCK)
    pad = nb * Q_BLOCK - n
    reach = window // dil

    def to_blocks(t):
        t = t.reshape(B, n, dil, H, dh).transpose(0, 2, 1, 3, 4)
        t = jnp.pad(t, ((0, 0), (0, 0), (0, pad), (0, 0), (0, 0)))
        return t.reshape(B, dil, nb, Q_BLOCK, H, dh)

    def with_prev(t):
        prev = jnp.pad(t, ((0, 0), (0, 0), (1, 0), (0, 0), (0, 0), (0, 0)))[:, :, :-1]
        return jnp.concatenate([prev, t], axis=3)

    qb = to_blocks(q)
    kb = with_prev(to_blocks(k))
    vb = with_prev(to_blocks(v))
    s = jnp.einsum('bgnqhd,bgnkhd->bgnhqk', qb, kb).astype(jnp.float32) * (dh ** -0.5)
    qi = jnp.arange(Q_BLOCK)[:, None]
    kj = jnp.arange(2 * Q_BLOCK)[None, :]
    dist = Q_BLOCK + qi - kj
    key_sub = jnp.arange(nb)[:, None, None] * Q_BLOCK + kj - Q_BLOCK
    valid = (dist >= 0) & (dist <= reach) & (key_sub >= 0)
    bias = -alibi_slopes(H)[:, None, None] * (dil * dist).astype(jnp.float32)
    s = jnp.where(valid[None, None, :, None], s + bias, -jnp.inf)
    m = jnp.max(s, axis=-1, keepdims=True)
    p = jnp.exp(s - m)
    l = jnp.sum(p, axis=-1, keepdims=True)
    o = jnp.einsum('bgnhqk,bgnkhd->bgnqhd', p / l, vb.astype(jnp.float32))
    lse = (m + jnp.log(l))[..., 0]
    o = o.reshape(B, dil, nb * Q_BLOCK, H, dh)[:, :, :n].transpose(0, 2, 1, 3, 4).reshape(B, S, H, dh)
    lse = lse.transpose(0, 1, 2, 4, 3).reshape(B, dil, nb * Q_BLOCK, H)[:, :, :n].transpose(0, 2, 1, 3).reshape(B, S, H)
    return o, lse

def dilated_attn_sample(q, kc, vc, window, dil):
    B, T, H, dh = q.shape
    L = kc.shape[1] - T
    steps = jnp.arange(window // dil + 1)
    idx = L + jnp.arange(T)[:, None] - dil * steps[None, :]
    valid = idx >= 0
    idx = jnp.maximum(idx, 0)
    kg = kc[:, idx]
    vg = vc[:, idx]
    s = jnp.einsum('bthd,btkhd->bthk', q, kg).astype(jnp.float32) * (dh ** -0.5)
    s = s - alibi_slopes(H)[:, None] * (dil * steps).astype(jnp.float32)[None, :]
    s = jnp.where(valid[None, :, None, :], s, -jnp.inf)
    m = jnp.max(s, axis=-1, keepdims=True)
    p = jnp.exp(s - m)
    l = jnp.sum(p, axis=-1, keepdims=True)
    o = jnp.einsum('bthk,btkhd->bthd', p / l, vg.astype(jnp.float32))
    lse = (m + jnp.log(l))[..., 0]
    return o, lse

def wkv_scan(r, decay, k, v, kk, a, s0):
    def step(S, inp):
        r_t, w_t, k_t, v_t, kk_t, a_t = inp
        sk = jnp.einsum('bhij,bhj->bhi', S, kk_t)
        S = S * w_t[:, :, None, :] - sk[..., None] * (kk_t * a_t)[:, :, None, :] + v_t[..., None] * k_t[:, :, None, :]
        return S, jnp.einsum('bhij,bhj->bhi', S, r_t)
    xs = tuple(jnp.swapaxes(t.astype(jnp.float32), 0, 1) for t in (r, decay, k, v, kk, a))
    s_final, out = lax.scan(step, s0.astype(jnp.float32), xs)
    return jnp.swapaxes(out, 0, 1), s_final

def trunk_layer(x, kv_bufs, shift0, wkv0, W):
    B, T, _ = x.shape
    x = half_swiglu(x, W['ffn1_norm'], W['ffn1_w_gate'], W['ffn1_w_up'], W['ffn1_w_down'])
    h = rmsnorm(x, W['mix_norm'])
    proj = h @ W['w_in']
    p_attn, p_shift, p_gate = jnp.split(proj, [ATTN_COLS, ATTN_COLS + SHIFT_COLS], axis=-1)

    qkv = p_attn.reshape(B, T, N_GROUPS, 3, ATTN_HEADS, HEAD_DIM)
    outs, lses, new_kv = [], [], []
    for gi, (window, dil) in enumerate(DILATED_GROUPS):
        q = rmsnorm(qkv[:, :, gi, 0], W['attn_q_norm'][gi])
        k = rmsnorm(qkv[:, :, gi, 1], W['attn_k_norm'][gi])
        v = qkv[:, :, gi, 2]
        kv = jnp.stack([k, v], axis=2)
        if kv_bufs is None:
            o, lse = dilated_attn_prompt(q, k, v, window, dil)
            new_kv.append(kv[:, -min(window, T):])
        else:
            kvc = jnp.concatenate([kv_bufs[gi].astype(kv.dtype), kv], axis=1)
            o, lse = dilated_attn_sample(q, kvc[:, :, 0], kvc[:, :, 1], window, dil)
            new_kv.append(kvc[:, -min(window, kvc.shape[1]):])
        outs.append(o)
        lses.append(lse)
    grp_w = jax.nn.softmax(jnp.stack(lses, axis=0), axis=0)
    o_attn = jnp.einsum('gbth,gbthd->bthd', grp_w, jnp.stack(outs, axis=0)).reshape(B, T, ATTN_WIDTH).astype(x.dtype)

    prev = jnp.concatenate([shift0[:, None].astype(p_shift.dtype), p_shift[:, :-1]], axis=1)
    u = p_shift + W['rwkv_mu'] * (prev - p_shift)
    r, k, v, uw, ua, ug = jnp.split(u, list(SHIFT_SPLITS), axis=-1)
    w_log = -jax.nn.softplus(-(W['rwkv_w0'] + jnp.tanh(uw) @ W['rwkv_w_lora_up'])) - 0.5
    decay = jnp.exp(-jnp.exp(w_log.astype(jnp.float32)))
    a = jax.nn.sigmoid(W['rwkv_a0'] + ua @ W['rwkv_a_lora_up'])
    g = jax.nn.sigmoid(ug) @ W['rwkv_g_lora_up']

    def heads(t):
        return t.reshape(B, T, RWKV_HEADS, HEAD_DIM)

    kk = heads(k * W['rwkv_k_k']).astype(jnp.float32)
    kk = kk * lax.rsqrt(jnp.sum(kk * kk, axis=-1, keepdims=True) + 1e-12)
    k = k * (1.0 + (a - 1.0) * W['rwkv_k_a'])
    r_h, k_h, v_h = heads(r).astype(jnp.float32), heads(k).astype(jnp.float32), heads(v).astype(jnp.float32)
    o, wkv_new = wkv_scan(r_h, heads(decay), k_h, v_h, kk, heads(a), wkv0)
    mean = jnp.mean(o, axis=-1, keepdims=True)
    var = jnp.mean(jnp.square(o - mean), axis=-1, keepdims=True)
    o = ((o - mean) * lax.rsqrt(var + LN_X_EPS)).reshape(B, T, RWKV_WIDTH) * W['rwkv_ln_gain'] + W['rwkv_ln_bias']
    bonus = jnp.sum(r_h * k_h * W['rwkv_r_k'], axis=-1, keepdims=True) * v_h
    o_rwkv = ((o + bonus.reshape(B, T, RWKV_WIDTH)) * g).astype(x.dtype)

    g_attn, g_rwkv = jnp.split(p_gate, 2, axis=-1)
    merged = jax.nn.sigmoid(g_attn) * (o_attn @ W['w_branch_attn']) + jax.nn.sigmoid(g_rwkv) * (o_rwkv @ W['w_branch_rwkv'])
    x = x + merged @ W['w_out']
    x = half_swiglu(x, W['ffn2_norm'], W['ffn2_w_gate'], W['ffn2_w_up'], W['ffn2_w_down'])
    return x, new_kv, p_shift[:, -1], wkv_new

def setup_inputs(seed: int = 0) -> dict:
    key = jax.random.key(seed)
    keys = iter(jax.random.split(key, 48))

    def normal(shape, scale):
        return jax.random.normal(next(keys), shape, jnp.float32) * scale

    def uniform(shape, lo, hi):
        return jax.random.uniform(next(keys), shape, jnp.float32, lo, hi)

    def gain(shape):
        return 1.0 + normal(shape, 0.02)

    Ld = DEPTH
    (w1, _), (w2, _), (w3, _) = DILATED_GROUPS
    return {
        'x_prompt': normal((BATCH, SEQ, D_MODEL), 1.0),
        'x_sample': normal((DEC_BATCH, DEC_SEQ, D_MODEL), 1.0),
        'cache_kv_w128': normal((Ld, DEC_BATCH, min(w1, PAST_LEN), 2, ATTN_HEADS, HEAD_DIM), 1.0),
        'cache_kv_w512': normal((Ld, DEC_BATCH, min(w2, PAST_LEN), 2, ATTN_HEADS, HEAD_DIM), 1.0),
        'cache_kv_w2048': normal((Ld, DEC_BATCH, min(w3, PAST_LEN), 2, ATTN_HEADS, HEAD_DIM), 1.0),
        'state_wkv': normal((Ld, DEC_BATCH, RWKV_HEADS, HEAD_DIM, HEAD_DIM), 0.3),
        'state_shift': normal((Ld, DEC_BATCH, SHIFT_COLS), 1.0),
        'ffn1_norm': gain((Ld, D_MODEL)),
        'ffn1_w_gate': normal((Ld, D_MODEL, D_FF), D_MODEL ** -0.5),
        'ffn1_w_up': normal((Ld, D_MODEL, D_FF), D_MODEL ** -0.5),
        'ffn1_w_down': normal((Ld, D_FF, D_MODEL), D_FF ** -0.5),
        'mix_norm': gain((Ld, D_MODEL)),
        'w_in': normal((Ld, D_MODEL, IN_COLS), D_MODEL ** -0.5),
        'attn_q_norm': gain((Ld, N_GROUPS, HEAD_DIM)),
        'attn_k_norm': gain((Ld, N_GROUPS, HEAD_DIM)),
        'rwkv_mu': uniform((Ld, SHIFT_COLS), 0.0, 1.0),
        'rwkv_w0': uniform((Ld, RWKV_WIDTH), -4.0, -0.5),
        'rwkv_w_lora_up': normal((Ld, DECAY_LORA, RWKV_WIDTH), 0.5 * DECAY_LORA ** -0.5),
        'rwkv_a0': normal((Ld, RWKV_WIDTH), 0.1),
        'rwkv_a_lora_up': normal((Ld, ICLR_LORA, RWKV_WIDTH), ICLR_LORA ** -0.5),
        'rwkv_g_lora_up': normal((Ld, GATE_LORA, RWKV_WIDTH), GATE_LORA ** -0.5),
        'rwkv_k_k': 0.85 + normal((Ld, RWKV_WIDTH), 0.02),
        'rwkv_k_a': gain((Ld, RWKV_WIDTH)),
        'rwkv_r_k': normal((Ld, RWKV_HEADS, HEAD_DIM), 0.5),
        'rwkv_ln_gain': gain((Ld, RWKV_WIDTH)),
        'rwkv_ln_bias': normal((Ld, RWKV_WIDTH), 0.02),
        'w_branch_attn': normal((Ld, ATTN_WIDTH, D_MODEL), ATTN_WIDTH ** -0.5),
        'w_branch_rwkv': normal((Ld, RWKV_WIDTH, D_MODEL), RWKV_WIDTH ** -0.5),
        'w_out': normal((Ld, D_MODEL, D_MODEL), D_MODEL ** -0.5),
        'ffn2_norm': gain((Ld, D_MODEL)),
        'ffn2_w_gate': normal((Ld, D_MODEL, D_FF), D_MODEL ** -0.5),
        'ffn2_w_up': normal((Ld, D_MODEL, D_FF), D_MODEL ** -0.5),
        'ffn2_w_down': normal((Ld, D_FF, D_MODEL), D_FF ** -0.5),
    }

def reference(x_prompt, x_sample, cache_kv_w128, cache_kv_w512, cache_kv_w2048, state_wkv, state_shift,
              ffn1_norm, ffn1_w_gate, ffn1_w_up, ffn1_w_down, mix_norm, w_in, attn_q_norm, attn_k_norm,
              rwkv_mu, rwkv_w0, rwkv_w_lora_up, rwkv_a0, rwkv_a_lora_up, rwkv_g_lora_up, rwkv_k_k, rwkv_k_a,
              rwkv_r_k, rwkv_ln_gain, rwkv_ln_bias, w_branch_attn, w_branch_rwkv, w_out,
              ffn2_norm, ffn2_w_gate, ffn2_w_up, ffn2_w_down):
    y_prompt, y_sample = x_prompt, x_sample
    bp = x_prompt.shape[0]
    new_p, new_s = [], []
    for l in range(DEPTH):
        W = dict(ffn1_norm=ffn1_norm[l], ffn1_w_gate=ffn1_w_gate[l], ffn1_w_up=ffn1_w_up[l], ffn1_w_down=ffn1_w_down[l],
                 mix_norm=mix_norm[l], w_in=w_in[l], attn_q_norm=attn_q_norm[l], attn_k_norm=attn_k_norm[l],
                 rwkv_mu=rwkv_mu[l], rwkv_w0=rwkv_w0[l], rwkv_w_lora_up=rwkv_w_lora_up[l], rwkv_a0=rwkv_a0[l],
                 rwkv_a_lora_up=rwkv_a_lora_up[l], rwkv_g_lora_up=rwkv_g_lora_up[l], rwkv_k_k=rwkv_k_k[l],
                 rwkv_k_a=rwkv_k_a[l], rwkv_r_k=rwkv_r_k[l], rwkv_ln_gain=rwkv_ln_gain[l], rwkv_ln_bias=rwkv_ln_bias[l],
                 w_branch_attn=w_branch_attn[l], w_branch_rwkv=w_branch_rwkv[l], w_out=w_out[l],
                 ffn2_norm=ffn2_norm[l], ffn2_w_gate=ffn2_w_gate[l], ffn2_w_up=ffn2_w_up[l], ffn2_w_down=ffn2_w_down[l])
        shift0 = jnp.zeros((bp, SHIFT_COLS), x_prompt.dtype)
        wkv0 = jnp.zeros((bp, RWKV_HEADS, HEAD_DIM, HEAD_DIM), jnp.float32)
        y_prompt, kv_p, sh_p, wkv_p = trunk_layer(y_prompt, None, shift0, wkv0, W)
        y_sample, kv_s, sh_s, wkv_s = trunk_layer(
            y_sample, (cache_kv_w128[l], cache_kv_w512[l], cache_kv_w2048[l]), state_shift[l], state_wkv[l], W)
        new_p.append((kv_p[0], kv_p[1], kv_p[2], wkv_p, sh_p))
        new_s.append((kv_s[0], kv_s[1], kv_s[2], wkv_s, sh_s))
    kv128_p = jnp.stack([st[0] for st in new_p])
    kv512_p = jnp.stack([st[1] for st in new_p])
    kv2048_p = jnp.stack([st[2] for st in new_p])
    wkv_p = jnp.stack([st[3] for st in new_p])
    shift_p = jnp.stack([st[4] for st in new_p])
    kv128_s = jnp.stack([st[0] for st in new_s])
    kv512_s = jnp.stack([st[1] for st in new_s])
    kv2048_s = jnp.stack([st[2] for st in new_s])
    wkv_s = jnp.stack([st[3] for st in new_s])
    shift_s = jnp.stack([st[4] for st in new_s])
    return (y_prompt, y_sample, kv128_p, kv512_p, kv2048_p, wkv_p, shift_p, kv128_s, kv512_s, kv2048_s, wkv_s, shift_s)


_drawn_inputs = setup_inputs


def setup_inputs(seed=0):
    import zlib

    import numpy as np

    out = dict(_drawn_inputs(seed))
    spreads = {}
    factors = {'ffn1_norm': 4.853,
     'attn_q_norm': 200.0,
     'attn_k_norm': 29.733,
     'rwkv_k_k': 157.818,
     'rwkv_k_a': 2.674,
     'rwkv_ln_gain': 60.456,
     'rwkv_ln_bias': 60.65,
     'ffn2_norm': 21.651}
    for name, (base, spread) in spreads.items():
        noise = np.random.default_rng([zlib.crc32(name.encode()), seed]).standard_normal(out[name].shape)
        drawn = base * np.exp(spread * noise) if base else spread * noise
        out[name] = __import__('jax').numpy.asarray(drawn.astype(out[name].dtype))
    for name, factor in factors.items():
        out[name] = (out[name] * factor).astype(out[name].dtype)
    return out
```

```python
from contextlib import ExitStack

import numpy as np
import concourse.bass as bass
from concourse import mybir

F32 = mybir.dt.float32
F32R = mybir.dt.float32r
ALU = mybir.AluOpType
ACT = mybir.ActivationFunctionType
AX = mybir.AxisListType

D, FF = 1024, 2816
SEQ, DB, DS = 512, 8, 8
NS = DB * DS
NT = SEQ + NS
HC = NT // 2
KD = D // 128
NF = FF // 128
HALF = NF // 2
CT = 4
DH = 64
SHT = 14
GROUPS = ((128, 1), (512, 4), (2048, 16))
PASTS = (128, 512, 1024)
RMS_EPS, KK_EPS, LN_EPS = 1e-6, 1e-12, 64e-5
C0 = float(np.exp(-0.5))
CH = 64
NCH = SEQ // CH
NEG = -3.0e37
CK = (128, 512, 512)
KOFF = (0, 320, 832)
NKEY = 1344
CTILE = (0, 1, 5, 9)

W8, W11 = KD * 128, HALF * 128
P_FFN1, P_RW, P_CT, P_ATT, P_MRG, P_OUT, P_FFN2 = 0, 30, 31, 37, 55, 67, 71
N_PAIR = 101
N_W8 = 2 * 44 + 2 + 12 + 36 + 24 + 8 + 2

COLS = {}
_n = 0
for _name, _w in (("g1", 8), ("gm", 8), ("g2", 8), ("mu", 14), ("w0", 4), ("a0", 4), ("kk", 4), ("ka", 4), ("rk", 4),
                  ("lng", 4), ("lnb", 4), ("qg", 3), ("kg", 3), ("slp", 8), ("sls", 4), ("eps", 3)):
    COLS[_name] = _n
    _n += _w
NPAR = _n

KCOL = {}
_n = 0
for _name, _w in (("ident", 128), ("ones", 128), ("bones", 128), ("m2T", 128), ("m2", 128), ("m4", 128), ("m8", 128),
                  ("m16", 128), ("m32", 128), ("m64", 128), ("SU", 128), ("IU", 128), ("SU8", 64), ("IU8", 64),
                  ("seq", 8), ("reset", NT)):
    KCOL[_name] = (_n, _w)
    _n += _w
NCONST = _n
LEVELS = ("m4", "m8", "m16", "m32", "m64")
NMASK = 256 + 512 + 512 + NKEY


def constants():
    c = np.zeros((128, NCONST), np.float32)

    def put(name, a):
        o, w = KCOL[name]
        c[:a.shape[0], o:o + w] = a

    r = np.arange(128)
    t, s = r[:, None], r[None, :]
    put("ident", np.eye(128))
    put("ones", np.ones((128, 128)))
    put("bones", (t // 64 == s // 64))
    for b in (2, 4, 8, 16, 32, 64):
        m = (t // b == s // b) & (t % b >= b // 2) & (s % b < b // 2)
        put("m%d" % b, m)
        if b == 2:
            put("m2T", m.T)
    put("SU", (t // CH == s // CH) & (t < s))
    put("IU", (t // CH == s // CH) & (t <= s))
    t, s = t[:64], s[:, :64]
    put("SU8", (t // DS == s // DS) & (t < s))
    put("IU8", (t // DS == s // DS) & (t <= s))
    put("seq", (np.arange(64)[:, None] // DS == np.arange(8)[None, :]))
    reset = np.ones(NT)
    reset[0:SEQ:CH] = 0
    reset[SEQ::DS] = 0
    put("reset", np.broadcast_to(reset, (128, NT)))

    m = np.zeros((128, NMASK), np.float32)
    q = np.arange(128)[:, None]

    def negdist(dist, ok):
        return np.where(ok, -dist, NEG)

    k = np.arange(256)[None, :]
    d = 128 + q - k
    m[:, 0:256] = negdist(d, (d >= 0) & (d <= 128))
    k = np.arange(512)[None, :] - 384
    d = q - k
    for g, o in ((1, 256), (2, 768)):
        m[:, o:o + 512] = negdist(d, (d >= 0) & (d % GROUPS[g][1] == 0) & (d <= GROUPS[g][0]))
    row = np.arange(128)
    b, tt = (row // 16)[:, None], (row % 8)[:, None]
    o = 1280
    for g in range(3):
        p = sample_positions(g)[None, :]
        d = PASTS[g] + tt - p
        m[:, o + KOFF[g]:o + KOFF[g] + CK[g]] = negdist(d, (d % GROUPS[g][1] == 0) & (d <= GROUPS[g][0]))
        kb, kt = (np.arange(64) // 8)[None, :], (np.arange(64) % 8)[None, :]
        d = tt - kt
        m[:, o + 128 + 64 * g:o + 192 + 64 * g] = negdist(d, (kb == b) & (d >= 0) & (d % GROUPS[g][1] == 0))
    return c, m


def sample_positions(g):
    p = np.arange(PASTS[g])
    return p if g < 2 else p[p % 16 < DS]


class Own:

    def __init__(self, eng, sem):
        self.eng, self.sem, self.base, self.k = eng, sem, 0, 0

    def __call__(self, ins):
        ins.then_inc(self.sem, 1)
        self.k += 1
        self.eng.wait_ge(self.sem, self.base + self.k)

    def enter(self, i, per):
        self.saved, self.per = self.base + self.k, per
        self.base, self.k = self.saved + i * per, 0

    def leave(self, count):
        assert self.k == self.per, (self.k, self.per)
        self.base, self.k = self.saved + count * self.per, 0


def build(nc, t):
    ctx = ExitStack()
    sems = {}

    def sem(name):
        if name not in sems:
            sems[name] = ctx.enter_context(nc.semaphore(name))
        return sems[name]

    def sb(c, name, shape, dt=F32):
        return c.enter_context(nc.sbuf_tensor(name, shape, dt))

    with ctx:
        x = sb(ctx, "x", [128, KD, NT])
        h_hi, h_lo = sb(ctx, "h_hi", [128, KD, NT], F32R), sb(ctx, "h_lo", [128, KD, NT], F32R)
        w_raw = [sb(ctx, "w_raw%d" % i, [128, W11]) for i in range(2)]
        w_hi = [sb(ctx, "w_hi%d" % i, [128, W11], F32R) for i in range(2)]
        w_lo = [sb(ctx, "w_lo%d" % i, [128, W11], F32R) for i in range(2)]
        par = sb(ctx, "par", [128, NPAR, 1])
        con = sb(ctx, "con", [128, NCONST])
        ps = ctx.enter_context(nc.psum_tensor("ps", [128, 8, 512], F32))

        def K(name, rows=128):
            o, w = KCOL[name]
            return con[0:rows, o:o + w]

        def P1(name, i=0):
            return par[:, COLS[name] + i]

        with ExitStack() as c:
            g_hi, g_lo = sb(c, "g_hi", [128, HALF, NT], F32R), sb(c, "g_lo", [128, HALF, NT], F32R)
            sg, gt = sb(c, "sg", [128, NT]), sb(c, "gt", [128, NT])
        with ExitStack() as c:
            sq = [sb(c, "sq%d" % i, [128, NT]) for i in range(2)]
            nrx, nry, nrt = (sb(c, n, [128, NT]) for n in ("nrx", "nry", "nrt"))
            hf = [sb(c, "hf%d" % i, [128, NT]) for i in range(2)]
        mid = ExitStack()
        o_rw = sb(mid, "o_rw", [128, CT, NT])
        with ExitStack() as c:
            PR = [sb(c, "praw%d" % i, [128, NT]) for i in range(2)]
            UR, UK = sb(c, "u_r", [128, NT]), sb(c, "u_k", [128, NT])
            UW, UG = sb(c, "u_wa", [128, NT]), sb(c, "u_g", [128, NT])
            SW, AA, CC, CX = (sb(c, n, [128, NT]) for n in ("sw", "aa", "cum", "cumx"))
            EP, EM, TT = (sb(c, n, [128, NT]) for n in ("exp_p", "exp_m", "tmp"))
            FM = sb(c, "fm", [128, 5, NT])
            KA, BH, KH, RH, UV = (FM[:, i] for i in range(5))
            TOK = sb(c, "tok", [128, 4, 4, 128])
            LR, LM, ZZ, XX, XT = ([sb(c, "%s%d" % (n, h), [128, 512]) for h in range(2)]
                                  for n in ("lraw", "lmask", "zz", "xx", "xt"))
            MV, W1 = sb(c, "mv", [128, 4, 128]), sb(c, "w1", [128, 4, 128])
            XK, UU = sb(c, "xk", [128, 512]), sb(c, "uu", [128, 4, 128])
            ST, STP = sb(c, "st", [128, NCH + 1, DH]), sb(c, "stp", [128, DH])
            BN = sb(c, "bonus", [128, CT, NT])
            LO = [sb(c, "lora%d" % i, [128, 128]) for i in range(2)]
            SV, SVP = sb(c, "sv", [128, CT, 5, NS]), sb(c, "svp", [128, CT, DB])
            SH, SH0 = sb(c, "sh", [128, SHT, 9]), sb(c, "sh0", [128, SHT, DB])
            GL = sb(c, "gl", [128, 512])
        o_at = sb(mid, "o_at", [128, CT, NT])
        with ExitStack() as c:
            QKV = sb(c, "qkv", [128, 3, 3, NT])
            asq, arx, ary, art = (sb(c, n, [128, NT]) for n in ("asq", "arx", "ary", "art"))
            VT = sb(c, "vtok", [128, 3, 4, 128])
            VS = sb(c, "vsam", [64, 3, 128])
            SB = [sb(c, "scores%d" % i, [128, NKEY]) for i in range(2)]
            PT = sb(c, "pt", [128, 12, 128])
            MSK = sb(c, "amask", [128, NMASK])
            QB = sb(c, "qblk", [128, 3, DB, 32])
            QA = sb(c, "qall", [128, 3, 128])
            KC = [sb(c, "kc%d" % i, [128, 1152]) for i in range(2)]
            VC = [sb(c, "vc%d" % i, [128, 9, 128]) for i in range(2)]
            OA = sb(c, "oa", [128, 4, 128])
            mx, ls = sb(c, "mx", [128, 2, 1]), sb(c, "ls", [128, 2, 1])
        with ExitStack() as c:
            o_hi, o_lo = sb(c, "o_hi", [128, 2 * CT, NT], F32R), sb(c, "o_lo", [128, 2 * CT, NT], F32R)
            m_hi, m_lo = sb(c, "m_hi", [128, KD, NT], F32R), sb(c, "m_lo", [128, KD, NT], F32R)
            sA, sR, mA = (sb(c, n, [128, NT]) for n in ("sig_a", "sig_r", "mrg"))
        mid.close()
        def flat(a):
            return a[:, :, :].rearrange("p t n -> p (t n)")

        SLR, SLM, SZZ, SXX, SXT, SNK, SMK, SNB, SMV, SW1 = (a[0:64, :] for a in (
            LR[0], LM[0], ZZ[0], XX[0], XT[0], LM[1], ZZ[1], LR[1], XX[1], XT[1]))
        SUU = flat(W1)[0:64]
        TOS = [a[0:64, 0:512] for a in (CC, CX, EM, EP)]
        SPREAD = [[a[0:64, 0:512] for a in p] for p in ((UR, UK), (PR[0], PR[1]))]
        SXK, SU0 = XK[:, 0:256], SW[:, 0:256]
        SST = TOK[:, :, :, :].rearrange("p a t n -> p a (t n)")

        unit_done, hi_done, lo_done = sem("unit_done"), sem("hi_done"), sem("lo_done")
        loaded = [sem("w_loaded_even"), sem("w_loaded_odd")]
        evac = [sem("set0_evacuated"), sem("set1_evacuated")]

        def bank2(b):
            return ps[:, b:b + 2, 0:HC]

        def two(a):
            return a.rearrange("p (c n) -> p c n", c=2)

        def load_unit(sp, P, par_, src, words):
            if not (isinstance(P, int) and P == 0):
                sp.wait_ge(lo_done, 2 * P - 1 + par_)
            sp.dma_start(w_raw[par_][:, 0:words], src).then_inc(loaded[par_], 16)

        def split_hi(act, P, par_, words):
            act.wait_ge(loaded[par_], 16 * (P + 1))
            if not (isinstance(P, int) and P == 0):
                act.wait_ge(unit_done, 2 * P - 1 + par_)
            nc.scalar.activation(w_hi[par_][:, 0:words], w_raw[par_][:, 0:words], ACT.Copy).then_inc(hi_done, 1)
            act.drain()

        def split_lo(pool, P, par_, words):
            pool.wait_ge(hi_done, 2 * P + par_ + 1)
            nc.gpsimd.tensor_tensor(w_lo[par_][:, 0:words], w_raw[par_][:, 0:words],
                                    w_hi[par_][:, 0:words].bitcast(F32), ALU.subtract).then_inc(lo_done, 1)

        def unit_wait(pe, P, par_):
            pe.wait_ge(lo_done, 2 * P + par_ + 1)
            if not (isinstance(P, int) and P == 0):
                pe.wait_ge(evac[par_], P)

        def three_pass(par_, a_hi, a_lo, k0, nk, b):
            for k in range(nk):
                wk = slice((k0 + k) * 128, (k0 + k + 1) * 128)
                for w, a, first, end in ((w_hi, a_hi, True, False), (w_hi, a_lo, False, False), (w_lo, a_hi, False, True)):
                    for c in range(2):
                        last = nc.tensor.matmul(ps[:, b + c, 0:HC], w[par_][:, wk], a[:, k, c * HC:(c + 1) * HC],
                                                start=(first and k == 0), stop=(end and k == nk - 1))
            return last

        def unit(pe, P, par_, a_hi=h_hi, a_lo=h_lo, nk=KD):
            unit_wait(pe, P, par_)
            three_pass(par_, a_hi, a_lo, 0, nk, 2 * par_).then_inc(unit_done, 1)

        def barrier(eng, n):
            eng.drain().then_inc(sem("phase%d_over" % n), 1)
            eng.wait_ge(sem("phase%d_over" % n), 3)

        def rsqrt_act(own, src, rx, ry, scale, eps):
            own(nc.scalar.activation(two(rx), src, ACT.Identity, bias=P1("eps", eps), scale=scale))
            own(nc.scalar.activation(ry, rx, ACT.Ln))
            nc.scalar.activation(ry, ry, ACT.Exp, scale=-0.5).then_inc(sem("rsqrt_guess"), 1)
            own.eng.drain()

        def rsqrt_dve(own, dve, n, rx, ry, rt):
            dve.wait_ge(sem("rsqrt_guess"), n)
            own(nc.vector.tensor_tensor(rt, ry, ry, ALU.mult))
            own(nc.vector.scalar_tensor_tensor(rt, rt, -0.5, rx, ALU.mult, ALU.mult))
            own(nc.vector.scalar_tensor_tensor(ry, rt, 1.5, ry, ALU.add, ALU.mult))

        RS_NORM = (0, 1, 1 + CT + 2 * CT + 24)
        RS_CT, RS_FIN, RS_ATT = 2, 2 + CT, 2 + 2 * CT
        RS_NORM = (0, 1, 2 + 2 * CT + 24)

        def norm_pe(pe, m):
            for k in range(KD):
                pe.wait_ge(sem("sq_ready"), 8 * m + k + 1)
                for c in range(2):
                    last = nc.tensor.matmul(ps[:, 4 + c, 0:HC], K("ones"), sq[k % 2][:, c * HC:(c + 1) * HC],
                                            start=(k == 0), stop=(k == KD - 1))
                last.then_inc(sem("sq_summed"), 1)

        def norm_act(act, own, m):
            if m == 0:
                act.wait_ge(sem("x_loaded"), 48)
            for k in range(KD):
                if 8 * m + k >= 2:
                    act.wait_ge(sem("sq_summed"), 8 * m + k - 1)
                nc.scalar.activation(sq[k % 2][:, :], x[:, k, :], ACT.Square).then_inc(sem("sq_ready"), 1)
                act.drain()
            act.wait_ge(sem("sq_summed"), 8 * m + 8)
            rsqrt_act(own, bank2(4), nrx[:, :], nry[:, :], 1.0 / D, 0)
            for k in range(KD):
                act.wait_ge(sem("hf_ready"), 8 * m + k + 1)
                nc.scalar.activation(h_hi[:, k, :], hf[k % 2][:, :], ACT.Copy).then_inc(sem("h_hi_ready"), 1)
                act.drain()

        def norm_dve(dve, own, m, gain):
            rsqrt_dve(own, dve, RS_NORM[m] + 1, nrx[:, :], nry[:, :], nrt[:, :])

            def low(k):
                dve.wait_ge(sem("h_hi_ready"), 8 * m + k + 1)
                nc.vector.tensor_tensor(h_lo[:, k, :], hf[k % 2][:, :], h_hi[:, k, :].bitcast(F32),
                                        ALU.subtract).then_inc(sem("h_ready"), 1)
                dve.drain()

            for k in range(KD):
                nc.vector.scalar_tensor_tensor(hf[k % 2][:, :], x[:, k, :], P1(gain, k), nry[:, :],
                                               ALU.mult, ALU.mult).then_inc(sem("hf_ready"), 1)
                dve.drain()
                if k:
                    low(k - 1)
            low(KD - 1)

        def ffn_pe(pe, f, P0):
            pe.wait_ge(sem("h_ready"), 8 * (2 * f + 1))
            with pe.Fori(0, 2) as half:
                with pe.Fori(0, HALF) as j:
                    P = P0 + 15 * half + j
                    unit(pe, P, 0)
                    unit(pe, P, 1)
                with pe.Fori(0, 4) as j:
                    P = P0 + 15 * half + HALF + j
                    pe.wait_ge(sem("g_ready"), HALF * (2 * f + half + 1))
                    unit(pe, P, 0, g_hi, g_lo, HALF)
                    unit(pe, P, 1, g_hi, g_lo, HALF)

        def ffn_act(act, f, P0):
            def pair(P, G, j, words):
                act.wait_ge(unit_done, 2 * P + 1)
                act.wait_ge(evac[1], P)
                nc.scalar.activation(two(sg[:, :]), bank2(0), ACT.Silu).then_inc(evac[0], 1)
                act.drain()
                split_hi(act, P + 1, 0, words)
                split_hi(act, P + 1, 1, words)
                act.wait_ge(evac[1], P + 1)
                nc.scalar.activation(g_hi[:, j, :], gt[:, :], ACT.Copy).then_inc(sem("g_hi_ready"), 1)
                act.drain()

            with act.Fori(0, 2) as half:
                with act.Fori(0, HALF - 1) as j:
                    pair(P0 + 15 * half + j, 0, j, W8)
                pair(P0 + 15 * half + HALF - 1, 0, HALF - 1, W11)
                with act.Fori(0, 3) as j:
                    split_hi(act, P0 + 15 * half + HALF + 1 + j, 0, W11)
                    split_hi(act, P0 + 15 * half + HALF + 1 + j, 1, W11)
                split_hi(act, P0 + 15 * half + 15, 0, W8)
                split_hi(act, P0 + 15 * half + 15, 1, W8)

        def ffn_dve(dve, f, P0):
            with dve.Fori(0, 2) as half:
                with dve.Fori(0, HALF) as j:
                    P, G = P0 + 15 * half + j, HALF * (2 * f + half) + j
                    dve.wait_ge(unit_done, 2 * P + 2)
                    dve.wait_ge(evac[0], P + 1)
                    nc.vector.tensor_tensor(two(gt[:, :]), two(sg[:, :]), bank2(2), ALU.mult).then_inc(evac[1], 1)
                    dve.drain()
                    dve.wait_ge(evac[1], P + 1)
                    dve.wait_ge(sem("g_hi_ready"), G + 1)
                    nc.vector.tensor_tensor(g_lo[:, j, :], gt[:, :], g_hi[:, j, :].bitcast(F32),
                                            ALU.subtract).then_inc(sem("g_ready"), 1)
                    dve.drain()
                with dve.Fori(0, 4) as j:
                    P = P0 + 15 * half + HALF + j
                    for q in range(2):
                        dve.wait_ge(unit_done, 2 * P + q + 1)
                        dve.wait_ge(evac[q], P)
                        nc.vector.scalar_tensor_tensor(two(x[:, 2 * j + q, :]), bank2(2 * q), 0.5, two(x[:, 2 * j + q, :]),
                                                       ALU.mult, ALU.add).then_inc(evac[q], 1)
                        dve.drain()

        def ffn_pool(pool, P0):
            with pool.Fori(0, 2) as half:
                with pool.Fori(0, HALF) as j:
                    for q in range(2):
                        split_lo(pool, P0 + 15 * half + j, q, W8)
                with pool.Fori(0, 4) as j:
                    for q in range(2):
                        split_lo(pool, P0 + 15 * half + HALF + j, q, W11)

        def ffn_sp(sp, P0, w8_0, w11_0):
            def some(half, j0, j1, down):
                def one(j):
                    for q in range(2):
                        if down:
                            load_unit(sp, P0 + 15 * half + HALF + j, q, t["w11"][w11_0 + 8 * half + 2 * j + q], W11)
                        else:
                            load_unit(sp, P0 + 15 * half + j, q, t["w8"][w8_0 + 22 * half + 2 * j + q], W8)
                with sp.Fori(j0, j1) as j:
                    one(j)

            if P0 == 0:
                for q in range(2):
                    load_unit(sp, 0, q, t["w8"][q], W8)
                some(0, 1, HALF, False)
                some(0, 0, 4, True)
                some(1, 0, HALF, False)
                some(1, 0, 4, True)
            else:
                with sp.Fori(0, 2) as half:
                    some(half, 0, HALF, False)
                    some(half, 0, 4, True)

        B5 = lambda P, q: 2 * P + q + 1
        PRODS = ["A", "D"] + ["A", "D", "D"] * 4 + ["A", "D"] + ["D", "D", "D"]
        NPROD = len(PRODS)
        N_A, N_D = PRODS.count("A"), PRODS.count("D")

        def rw_units(i):
            return [(P_CT + 3 * i[0] + (3 * i[1] + n) // 2, (3 * i[1] + n) % 2, n) for n in range(3)]

        def tile_of(a, T, h):
            return a[64 * h:64 * h + 64, T * 128:(T + 1) * 128]

        def rwkv_pe(pe):
            pe.wait_ge(sem("h_ready"), 16)
            unit(pe, P_RW, 0)
            unit(pe, P_RW, 1)
            pe.wait_ge(sem("lora_in_ready"), 2)
            with pe.Fori(0, 2) as cc:
                for c2 in range(2):
                    ct = 2 * cc + c2
                    for P, q, n in rw_units((cc, c2)):
                        unit(pe, P, q)
                    pe.wait_ge(sem("lora_w%d" % c2), 16 * (cc + 1))
                    pe.wait_ge(sem("o_evac"), ct)
                    for r, b in ((0, 4), (1, 6)):
                        for c in range(2):
                            last = nc.tensor.matmul(ps[:, b + c, 0:HC], LO[c2][64 * r:64 * r + 64, :],
                                                    UW[64 * r:64 * r + 64, c * HC:(c + 1) * HC], start=True, stop=True)
                        last.then_inc(sem("lora_done"), 1)
                    pe.wait_ge(sem("kk_sq"), ct + 1)
                    pe.wait_ge(sem("gates_ready"), ct + 1)
                    for c in range(2):
                        last = nc.tensor.matmul(ps[:, 6 + c, 0:HC], K("bones"), TT[:, c * HC:(c + 1) * HC], start=True, stop=True)
                    last.then_inc(sem("kk_norm"), 1)
                    for a, arr, need in ((0, KA, 1), (1, BH, 2), (2, KH, 3), (3, UV, 4)):
                        pe.wait_ge(sem("fm_ready"), 4 * ct + need)
                        if a == 2:
                            pe.wait_ge(sem("rsqrt_guess"), RS_CT + ct + 1)
                        for T in range(4):
                            last = nc.tensor.transpose(ps[:, 4 + a, T * 128:(T + 1) * 128], arr[:, T * 128:(T + 1) * 128], K("ident"))
                        last.then_inc(sem("tr_done"), 1)
                    pe.wait_ge(sem("rk_ready"), ct + 1)
                    pe.wait_ge(sem("tok_a"), 2 * ct + 2)
                    for c in range(2):
                        last = nc.tensor.matmul(ps[:, 4 + c, 0:HC], K("bones"), TT[:, c * HC:(c + 1) * HC], start=True, stop=True)
                    last.then_inc(sem("bonus_sum"), 1)
                    done_a, done_d = 0, 0
                    counts = []
                    for kind in PRODS:
                        done_a += kind == "A"
                        done_d += kind == "D"
                        counts.append((kind, done_a, done_d))

                    def bank_free(n, h):
                        if n == 0:
                            pe.wait_ge(sem("bonus_evac"), ct + 1)
                        elif n == 1:
                            pe.wait_ge(sem("tok_d"), 2 * ct + 2)
                        else:
                            read(n - 2, h)

                    def read(n, h):
                        kind, a, d = counts[n]
                        if kind == "A":
                            pe.wait_ge(sem("mat_a%d" % h), N_A * ct + a)
                        else:
                            pe.wait_ge(sem("mat_d%d" % h), N_D * ct + d)

                    def product(n, h, lhs, rhs):
                        for T in range(4):
                            last = nc.tensor.matmul(ps[:, 4 + (2 * n + h) % 4, T * 128:(T + 1) * 128], lhs(T), rhs(T),
                                                    start=True, stop=True)
                        last.then_inc(sem("mat_done%d" % h), 1)

                    def cols(a):
                        return lambda T: a[:, T * 128:(T + 1) * 128]

                    for h in range(2):
                        bank_free(0, h)
                        product(0, h, lambda T: tile_of(KA, T, h), lambda T: tile_of(BH, T, h))
                    for h in range(2):
                        bank_free(1, h)
                        product(1, h, lambda T: tile_of(BH, T, h), lambda T: tile_of(KA, T, h))
                    n = 2
                    for lv in range(5):
                        for h in range(2):
                            bank_free(n, h)
                            if lv == 0:
                                pe.wait_ge(sem("inv_init%d" % h), ct + 1)
                            else:
                                read(n - 1, h)
                                pe.wait_ge(sem("lm_ready%d" % h), 4 * ct + lv)
                            product(n, h, cols(LM[h]), cols(XT[h]))
                        if lv < 4:
                            for h in range(2):
                                read(n, h)
                                bank_free(n + 1, h)
                                product(n + 1, h, cols(ZZ[h]), cols(XX[h]))
                            for h in range(2):
                                bank_free(n + 2, h)
                                product(n + 2, h, cols(XX[h]), cols(ZZ[h]))
                            n += 3
                        else:
                            for h in range(2):
                                read(n, h)
                                bank_free(n + 1, h)
                                product(n + 1, h, cols(XX[h]), cols(ZZ[h]))
                            n += 2
                    for lhs, rhs in ((KH, KA), (BH, RH), (KH, RH)):
                        for h in range(2):
                            bank_free(n, h)
                            product(n, h, lambda T: tile_of(lhs, T, h), lambda T: tile_of(rhs, T, h))
                        n += 1
                    assert n == NPROD
                    for h in range(2):
                        read(NPROD - 3, h)
                        read(NPROD - 2, h)
                        for T in range(4):
                            last = nc.tensor.matmul(ps[:, 6, T * 128 + 64 * h:T * 128 + 64 * h + 64], ZZ[h][:, T * 128:(T + 1) * 128],
                                                    TOK[:, 3, T, 64 * h:64 * h + 64], start=True, stop=True)
                    last.then_inc(sem("mv_done"), 1)
                    for h in range(2):
                        read(NPROD - 1, h)
                        for T in range(4):
                            last = nc.tensor.matmul(ps[64 * h:64 * h + 64, 4, T * 128:(T + 1) * 128], TOK[:, 0, T, 64 * h:64 * h + 64],
                                                    XT[h][:, T * 128:(T + 1) * 128], start=True, stop=True)
                    last.then_inc(sem("xk_done"), 1)
                    pe.wait_ge(sem("mv_evac"), ct + 1)
                    for h in range(2):
                        for T in range(4):
                            last = nc.tensor.matmul(ps[:, 7, T * 128 + 64 * h:T * 128 + 64 * h + 64], XT[h][:, T * 128:(T + 1) * 128],
                                                    MV[:, T, 64 * h:64 * h + 64], start=True, stop=True)
                    last.then_inc(sem("w1_done"), 1)
                    pe.wait_ge(sem("xk_evac"), ct + 1)
                    pe.wait_ge(sem("w1_evac"), ct + 1)
                    for ch in range(NCH):
                        r0, T = 64 * (ch % 2), ch // 2
                        pe.wait_ge(sem("st_ready"), 1 + NCH * ct + ch)
                        for h in range(2):
                            last = nc.tensor.matmul(ps[:, 4 + h, 0:64], XK[64 * h:64 * h + 64, 128 * T:128 * T + 128],
                                                    ST[64 * h:64 * h + 64, ch, :], start=True, stop=True)
                        last.then_inc(sem("u_done"), 1)
                        nc.tensor.matmul(ps[:, 6, 0:128], TOK[r0:r0 + 64, 2, T, :], TOK[r0:r0 + 64, 3, T, :], start=True, stop=False)
                        pe.wait_ge(sem("u_ready"), NCH * ct + ch + 1)
                        last = nc.tensor.matmul(ps[:, 6, 0:128], TOK[r0:r0 + 64, 1, T, :], UU[r0:r0 + 64, T, :], start=False, stop=True)
                        last.then_inc(sem("ds_done"), 1)
                    for h in range(2):
                        rows = slice(64 * h, 64 * h + 64)
                        for T in range(4):
                            o = ps[rows, 7, T * 128:(T + 1) * 128]
                            nc.tensor.matmul(o, UU[:, T, rows], LR[h][:, T * 128:(T + 1) * 128], start=(T == 0), stop=False,
                                             skip_group_check=True)
                            nc.tensor.matmul(o, TOK[:, 3, T, rows], LM[h][:, T * 128:(T + 1) * 128], start=False, stop=False,
                                             skip_group_check=True)
                            for e in range(2):
                                ch = 2 * T + e
                                last = nc.tensor.matmul(ps[rows, 7, ch * 64:ch * 64 + 64], ST[rows, ch, :], RH[rows, ch * 64:ch * 64 + 64],
                                                        start=False, stop=True, skip_group_check=True)
                    last.then_inc(sem("o_done"), 1)

        def rwkv_act(act, own):
            def take(P, q, n, e, tile):
                act.wait_ge(unit_done, B5(P, q))
                if not (isinstance(e, int) and e < 2):
                    act.wait_ge(sem("mixed"), e - 1)
                nc.scalar.activation(two(PR[q][:, :]), bank2(2 * q), ACT.Copy).then_inc(evac[q], 1)
                act.drain()
                act.wait_ge(evac[q], P + 1)
                nc.scalar.activation(SH[:, tile, :], PR[q][:, SEQ - 1:NT:DS], ACT.Copy).then_inc(sem("shift_kept"), 1)
                act.drain()
                split_hi(act, P + 1, q, W8)

            take(P_RW, 0, 0, 0, 12)
            take(P_RW, 1, 1, 1, 13)
            act.wait_ge(sem("mixed"), 1)
            nc.scalar.activation(UW[0:64, :], UW[0:64, :], ACT.Tanh).then_inc(sem("lora_in_ready"), 1)
            act.drain()
            act.wait_ge(sem("mixed"), 2)
            nc.scalar.activation(UG[:, :], UG[:, :], ACT.Sigmoid).then_inc(sem("lora_in_ready"), 1)
            act.drain()
            with act.Fori(0, 2) as cc:
                own.enter(cc, 2 * 5)
                for c2 in range(2):
                    ct = 2 * cc + c2
                    for P, q, n in rw_units((cc, c2)):
                        take(P, q, n, 2 + 6 * cc + 3 * c2 + n, 4 * n + ct)
                    act.wait_ge(sem("lora_done"), 2 * ct + 1)
                    nc.scalar.activation(two(SW[:, :]), bank2(4), ACT.Sigmoid, bias=P1("w0", ct))
                    act.wait_ge(sem("lora_done"), 2 * ct + 2)
                    nc.scalar.activation(two(AA[:, :]), bank2(6), ACT.Sigmoid, bias=P1("a0", ct)).then_inc(sem("gates_ready"), 1)
                    act.drain()
                    act.wait_ge(sem("kkr_ready"), ct + 1)
                    nc.scalar.activation(TT[:, :], KA, ACT.Square).then_inc(sem("kk_sq"), 1)
                    act.drain()
                    act.wait_ge(sem("cum_ready"), ct + 1)
                    own(nc.scalar.activation(EP[:, :], CC[:, :], ACT.Exp, scale=-C0))
                    own(nc.scalar.activation(EM[:, :], CC[:, :], ACT.Exp, scale=C0))
                    nc.scalar.activation(CX[:, :], CX[:, :], ACT.Exp, scale=-C0).then_inc(sem("exps_ready"), 1)
                    act.drain()
                    act.wait_ge(sem("kk_norm"), ct + 1)
                    rsqrt_act(own, bank2(6), CC[:, :], SW[:, :], 1.0, 1)
                    for a in range(2):
                        act.wait_ge(sem("tr_done"), 4 * ct + a + 1)
                        nc.scalar.activation(TOK[:, a].rearrange("p t n -> p (t n)"), ps[:, 4 + a, :], ACT.Copy).then_inc(sem("tok_a"), 1)
                        act.drain()
                    act.wait_ge(sem("fm_ready"), 4 * ct + 4)
                    nc.scalar.activation(SV[:, ct], FM[:, :, SEQ:NT], ACT.Copy)
                    own(nc.scalar.activation(SVP[:, ct], EP[:, SEQ + DS - 1:NT:DS], ACT.Copy))
                    for h in range(2):
                        act.wait_ge(sem("mat_done%d" % h), NPROD * ct + 1)
                        nc.scalar.activation(LR[h][:, :], ps[:, 4 + h, :], ACT.Copy).then_inc(sem("mat_a%d" % h), 1)
                        act.drain()
                    for lv in range(5):
                        n = 2 + 3 * lv
                        for h in range(2):
                            act.wait_ge(sem("mat_done%d" % h), NPROD * ct + n + 1)
                            nc.scalar.activation(ZZ[h][:, :], ps[:, 4 + (2 * n + h) % 4, :], ACT.Copy).then_inc(sem("mat_a%d" % h), 1)
                            act.drain()
                    act.wait_ge(sem("mv_done"), ct + 1)
                    nc.scalar.activation(MV[:, :, :].rearrange("p t n -> p (t n)"), ps[:, 6, :], ACT.Copy).then_inc(sem("mv_evac"), 1)
                    act.drain()
                    act.wait_ge(sem("w1_done"), ct + 1)
                    nc.scalar.activation(W1[:, :, :].rearrange("p t n -> p (t n)"), ps[:, 7, :], ACT.Copy).then_inc(sem("w1_evac"), 1)
                    act.drain()
                    act.wait_ge(sem("st_ready"), 1 + NCH * ct + NCH)
                    act.dma_start(t["wkv_p"][ct], ST[:, NCH, :]).then_inc(sem("wkvp_stored"), 16)
                    act.wait_ge(sem("o_done"), ct + 1)
                    nc.scalar.activation(o_rw[:, ct, 0:SEQ], ps[:, 7, :], ACT.Copy).then_inc(sem("o_evac"), 1)
                    act.drain()
                own.leave(2)
            act.wait_ge(sem("shift_kept"), SHT)
            act.dma_start(t["shift"], SH[:, :, :]).then_inc(sem("shift_stored"), 16)

        def rwkv_dve(dve, own):
            V = nc.vector
            V.memset(ST[:, 0, :], 0.0).then_inc(sem("st_ready"), 1)
            dve.drain()
            dve.wait_ge(sem("rw_loaded"), 32)

            def mix(P, q, out, mu, tile):
                p = PR[q]
                dve.wait_ge(evac[q], P + 1)
                V.tensor_tensor(out[:, 1:SEQ], p[:, 0:SEQ - 1], p[:, 1:SEQ], ALU.subtract)
                V.tensor_scalar(out[:, 0:1], p[:, 0:1], -1.0, None, ALU.mult)
                s, so = (a[:, SEQ:NT].rearrange("p (b t) -> p b t", t=DS) for a in (p, out))
                V.tensor_tensor(so[:, :, 1:DS], s[:, :, 0:DS - 1], s[:, :, 1:DS], ALU.subtract)
                own(V.tensor_tensor(so[:, :, 0], SH0[:, tile, :], s[:, :, 0], ALU.subtract))
                V.scalar_tensor_tensor(out, out, mu, p[:, :], ALU.mult, ALU.add).then_inc(sem("mixed"), 1)
                dve.drain()

            mix(P_RW, 0, UW[:, :], P1("mu", 12), 12)
            mix(P_RW, 1, UG[:, :], P1("mu", 13), 13)
            with dve.Fori(0, 2) as cc:
                own.enter(cc, RW_OWN)
                for c2 in range(2):
                    ct = 2 * cc + c2
                    for (P, q, n), out in zip(rw_units((cc, c2)), (UR[:, :], UK[:, :], UV)):
                        mix(P, q, out, P1("mu", 4 * n + ct), 4 * n + ct)
                    dve.wait_ge(sem("mixed"), 2 + 3 * (ct + 1))
                    V.tensor_scalar(KA, UK[:, :], P1("kk", ct), None, ALU.mult).then_inc(sem("kkr_ready"), 1)
                    dve.drain()
                    dve.wait_ge(sem("gates_ready"), ct + 1)
                    own(V.tensor_tensor_scan(CC[:, :], K("reset"), SW[:, :], 0.0, ALU.mult, ALU.add))
                    V.tensor_tensor(CX[:, :], CC[:, :], SW[:, :], ALU.subtract).then_inc(sem("cum_ready"), 1)
                    dve.drain()
                    own(V.tensor_scalar(BH, AA[:, :], 1.0, P1("ka", ct), ALU.subtract, ALU.mult))
                    own(V.scalar_tensor_tensor(UK[:, :], BH, 1.0, UK[:, :], ALU.add, ALU.mult))
                    rsqrt_dve(own, dve, RS_CT + ct + 1, CC[:, :], SW[:, :], TT[:, :])
                    own(V.tensor_tensor(TT[:, :], KA, SW[:, :], ALU.mult))
                    dve.wait_ge(sem("exps_ready"), ct + 1)
                    V.tensor_tensor(KA, TT[:, :], CX[:, :], ALU.mult).then_inc(sem("fm_ready"), 1)
                    dve.drain()
                    own(V.tensor_tensor(TT[:, :], TT[:, :], AA[:, :], ALU.mult))
                    V.scalar_tensor_tensor(BH, TT[:, :], -1.0, EM[:, :], ALU.mult, ALU.mult).then_inc(sem("fm_ready"), 1)
                    dve.drain()
                    V.tensor_tensor(KH, UK[:, :], EM[:, :], ALU.mult).then_inc(sem("fm_ready"), 1)
                    dve.drain()
                    V.tensor_tensor(RH, UR[:, :], EP[:, :], ALU.mult).then_inc(sem("fm_ready"), 1)
                    dve.drain()
                    V.scalar_tensor_tensor(TT[:, :], UR[:, :], P1("rk", ct), UK[:, :], ALU.mult, ALU.mult).then_inc(sem("rk_ready"), 1)
                    dve.drain()
                    for a in range(2, 4):
                        dve.wait_ge(sem("tr_done"), 4 * ct + a + 1)
                        V.tensor_copy(TOK[:, a].rearrange("p t n -> p (t n)"), ps[:, 4 + a, :]).then_inc(sem("tok_d"), 1)
                        dve.drain()
                    dve.wait_ge(sem("bonus_sum"), ct + 1)
                    V.tensor_tensor(two(BN[:, ct]), bank2(4), two(UV), ALU.mult).then_inc(sem("bonus_evac"), 1)
                    dve.drain()

                    def by_tile(a):
                        return a.rearrange("p (t n) -> p t n", t=4)

                    def mask(name):
                        return K(name).unsqueeze(1).to_broadcast([128, 4, 128])

                    n_d = [0, 0]

                    def evac_d(h, ins):
                        ins.then_inc(sem("mat_d%d" % h), 1)
                        dve.drain()
                        n_d[h] += 1

                    def my(h):
                        dve.wait_ge(sem("mat_d%d" % h), N_D * ct + n_d[h])

                    for h in range(2):
                        dve.wait_ge(sem("mat_done%d" % h), NPROD * ct + 2)
                        evac_d(h, V.tensor_tensor(by_tile(XT[h][:, :]), by_tile(ps[:, 6 + h, :]), mask("m2T"), ALU.mult))
                        dve.wait_ge(sem("mat_a%d" % h), N_A * ct + 1)
                        own(V.tensor_tensor(by_tile(XX[h][:, :]), by_tile(LR[h][:, :]), mask("m2"), ALU.mult))
                        V.tensor_tensor(by_tile(XX[h][:, :]), by_tile(XX[h][:, :]), mask("ident"), ALU.add)
                        my(h)
                        V.tensor_tensor(by_tile(XT[h][:, :]), by_tile(XT[h][:, :]), mask("ident"), ALU.add)
                        V.tensor_tensor(by_tile(LM[h][:, :]), by_tile(LR[h][:, :]), mask(LEVELS[0]), ALU.mult)\
                            .then_inc(sem("inv_init%d" % h), 1)
                        dve.drain()
                    for lv in range(5):
                        n = 2 + 3 * lv
                        if lv < 4:
                            for h in range(2):
                                dve.wait_ge(sem("mat_done%d" % h), NPROD * ct + n + 1)
                                V.tensor_tensor(by_tile(LM[h][:, :]), by_tile(LR[h][:, :]), mask(LEVELS[lv + 1]), ALU.mult)\
                                    .then_inc(sem("lm_ready%d" % h), 1)
                                dve.drain()
                            for h in range(2):
                                dve.wait_ge(sem("mat_done%d" % h), NPROD * ct + n + 3)
                                if lv == 0:
                                    dve.wait_ge(sem("inv_init%d" % h), ct + 1)
                                else:
                                    my(h)
                                evac_d(h, V.tensor_tensor(XX[h][:, :], XX[h][:, :], ps[:, 4 + (2 * n + 2 + h) % 4, :], ALU.add))
                                evac_d(h, V.tensor_tensor(XT[h][:, :], XT[h][:, :], ps[:, 4 + (2 * n + 4 + h) % 4, :], ALU.add))
                        else:
                            for h in range(2):
                                dve.wait_ge(sem("mat_done%d" % h), NPROD * ct + n + 2)
                                my(h)
                                evac_d(h, V.tensor_tensor(XT[h][:, :], XT[h][:, :], ps[:, 4 + (2 * n + 2 + h) % 4, :], ALU.add))
                    for n, out, m in ((NPROD - 3, ZZ, "SU"), (NPROD - 2, LR, "IU"), (NPROD - 1, LM, "IU")):
                        for h in range(2):
                            dve.wait_ge(sem("mat_done%d" % h), NPROD * ct + n + 1)
                            evac_d(h, V.tensor_tensor(by_tile(out[h][:, :]), by_tile(ps[:, 4 + (2 * n + h) % 4, :]), mask(m), ALU.mult))
                    assert n_d == [N_D, N_D]
                    dve.wait_ge(sem("xk_done"), ct + 1)
                    V.tensor_copy(XK[:, :], ps[:, 4, :]).then_inc(sem("xk_evac"), 1)
                    dve.drain()
                    dve.wait_ge(sem("w1_evac"), ct + 1)
                    for ch in range(NCH):
                        r0, T = 64 * (ch % 2), ch // 2
                        end = EP[:, 64 * ch + 63:64 * ch + 64]
                        dve.wait_ge(sem("st_ready"), 1 + NCH * ct + ch)
                        own(V.tensor_scalar(STP[:, :], ST[:, ch, :], end, None, ALU.mult))
                        dve.wait_ge(sem("u_done"), NCH * ct + ch + 1)
                        V.tensor_tensor(UU[r0:r0 + 64, T, :].rearrange("p (h n) -> p h n", h=2), ps[r0:r0 + 64, 4:6, 0:64],
                                        W1[r0:r0 + 64, T, :].rearrange("p (h n) -> p h n", h=2), ALU.add)\
                            .then_inc(sem("u_ready"), 1)
                        dve.drain()
                        dve.wait_ge(sem("ds_done"), NCH * ct + ch + 1)
                        if ch == NCH - 1:
                            dve.wait_ge(sem("wkvp_stored"), 16 * ct)
                        for h in range(2):
                            r = slice(64 * h, 64 * h + 64)
                            ins = V.scalar_tensor_tensor(ST[r, ch + 1, :], ps[r, 6, r], end[r], STP[r, :], ALU.mult, ALU.add)
                        ins.then_inc(sem("st_ready"), 1)
                        dve.drain()
                own.leave(2)

        RW_OWN = 2 * (3 + 1 + 2 + 3 + 1 + 1 + 2 + NCH)

        HEADS = [(ct, h) for ct in range(CT) for h in range(2)]

        def hc(ct, h):
            return slice(128 * ct + 64 * h, 128 * ct + 64 * h + 64)

        def mc(ct, h):
            return slice(256 * h + 64 * ct, 256 * h + 64 * ct + 64)

        def rows_of(h):
            return slice(64 * h, 64 * h + 64)

        def rwsam_pe(pe):
            def heads(bank, lhs, rhs, where=mc):
                for ct, h in HEADS:
                    last = nc.tensor.matmul(ps[0:64, bank, where(ct, h)], lhs(ct, h), rhs(ct, h), start=True, stop=True)
                last.then_inc(sem("smat"), 1)

            def scores(bank, a, b):
                for ct, h in HEADS:
                    last = nc.tensor.matmul(ps[0:64, bank + h, 64 * ct:64 * ct + 64], SV[rows_of(h), ct, a, :], SV[rows_of(h), ct, b, :],
                                            start=True, stop=True)
                last.then_inc(sem("smat"), 1)

            def mm(a):
                return lambda ct, h: a[:, mc(ct, h)]

            def tm(a):
                return lambda ct, h: a[:, hc(ct, h)]

            for i, a in enumerate((0, 1, 2, 4)):
                for ct in range(CT):
                    last = nc.tensor.transpose(ps[0:64, 4 + i, 128 * ct:128 * ct + 128], SV[:, ct, a, :], K("ident"))
                last.then_inc(sem("s_tr"), 1)
            scores(0, 0, 1)
            scores(2, 1, 0)
            pe.wait_ge(sem("s_inv"), 1)
            pe.wait_ge(sem("s_tok_d"), 2)
            heads(6, mm(SLM), mm(SXT))
            pe.wait_ge(sem("s_act"), 2)
            heads(7, mm(SZZ), mm(SXX))
            heads(4, mm(SXX), mm(SZZ))
            pe.wait_ge(sem("s_inv"), 2)
            heads(6, mm(SLM), mm(SXT))
            pe.wait_ge(sem("s_act"), 3)
            heads(7, mm(SXX), mm(SZZ))
            scores(0, 2, 0)
            scores(2, 1, 3)
            scores(4, 2, 3)
            pe.wait_ge(sem("s_dve"), 1)
            pe.wait_ge(sem("s_dve"), 2)
            heads(7, mm(SMK), tm(TOS[3]), hc)
            pe.wait_ge(sem("s_dve"), 4)
            for ct, h in HEADS:
                last = nc.tensor.matmul(ps[rows_of(h), 5, 64 * ct:64 * ct + 64], TOS[0][:, hc(ct, h)], SXT[:, mc(ct, h)],
                                        start=True, stop=True)
            last.then_inc(sem("smat"), 1)
            pe.wait_ge(sem("s_act"), 4)
            heads(4, mm(SXT), tm(SMV), hc)
            pe.wait_ge(sem("s_dve"), 5)
            pe.wait_ge(sem("s_states"), 16)
            for ct, h in HEADS:
                for b in range(DB):
                    c = slice(64 * ct + 8 * b, 64 * ct + 8 * b + 8)
                    last = nc.tensor.matmul(ps[rows_of(h), 6, c], SST[rows_of(h), ct, 64 * b:64 * b + 64], SXK[rows_of(h), c],
                                            start=True, stop=True)
            last.then_inc(sem("smat"), 1)
            pe.wait_ge(sem("s_act"), 6)
            for ct in range(CT):
                last = nc.tensor.transpose(ps[0:64, 7, 128 * ct:128 * ct + 128], SU0[:, 64 * ct:64 * ct + 64], K("ident"))
            last.then_inc(sem("smat"), 1)
            pe.wait_ge(sem("s_dve"), 6)
            for h in range(2):
                for ct in range(CT):
                    o = ps[rows_of(h), 4, 64 * ct:64 * ct + 64]
                    nc.tensor.matmul(o, SUU[:, hc(ct, h)], SNB[:, mc(ct, h)], start=(ct == 0), stop=False, skip_group_check=True)
                    nc.tensor.matmul(o, TOS[3][:, hc(ct, h)], SNK[:, mc(ct, h)], start=False, stop=True, skip_group_check=True)
                    for b in range(DB):
                        c = slice(64 * ct + 8 * b, 64 * ct + 8 * b + 8)
                        last = nc.tensor.matmul(ps[rows_of(h), 0, c], SST[rows_of(h), ct, 64 * b:64 * b + 64],
                                                SV[rows_of(h), ct, 3, 8 * b:8 * b + 8], start=True, stop=True)
            last.then_inc(sem("smat"), 1)
            for ct, h in HEADS:
                pe.wait_ge(sem("s_spread"), 2 * ct + h + 1)
                if ct >= 2:
                    pe.wait_ge(sem("s_new"), ct - 1)
                o = ps[rows_of(h), 5 + ct % 2, :]
                nc.tensor.matmul(o, TOS[1][:, hc(ct, h)], SPREAD[h][0], start=True, stop=False)
                nc.tensor.matmul(o, TOS[2][:, hc(ct, h)], SPREAD[h][1], start=False, stop=True).then_inc(sem("s_dstate"), 1)

        def rwsam_act(act, own):
            def take(need, out, src):
                act.wait_ge(sem("smat"), need)
                nc.scalar.activation(out, src, ACT.Copy).then_inc(sem("s_act"), 1)
                act.drain()

            for i in range(2):
                act.wait_ge(sem("s_tr"), i + 1)
                nc.scalar.activation(TOS[i], ps[0:64, 4 + i, :], ACT.Copy).then_inc(sem("s_tok_a"), 1)
                act.drain()
            take(1, SLR.rearrange("p (h n) -> p h n", h=2), ps[0:64, 0:2, 0:256])
            take(3, SZZ, ps[0:64, 6, :])
            take(6, SZZ, ps[0:64, 6, :])
            take(11, SMV, ps[0:64, 7, :])
            take(13, SW1, ps[0:64, 4, :])
            take(14, SU0, ps[:, 6, 0:256])
            act.wait_ge(sem("smat"), 16)
            nc.scalar.activation(o_rw[:, :, SEQ:NT], ps[:, 4, 0:256].rearrange("p (c n) -> p c n", c=CT), ACT.Copy)\
                .then_inc(sem("o_new"), 1)
            act.drain()
            for ct in range(CT):
                act.wait_ge(sem("s_new"), ct + 1)
                act.dma_start(t["wkv_s"][ct], SST[:, ct, :]).then_inc(sem("wkvs_stored"), 16)

        def rwsam_dve(dve, own):
            V = nc.vector

            def by_head(a):
                return a.rearrange("p (h n) -> p h n", h=8)

            def mask(name):
                return K(name, 64)[:, 0:64].unsqueeze(1).to_broadcast([64, 8, 64])

            def by_pair(a):
                return a.rearrange("p (h c n) -> p h c n", h=2, c=CT)

            def score_banks(b):
                return ps[0:64, b:b + 2, 0:256].rearrange("p h (c n) -> p h c n", c=CT)

            def mask4(name):
                return K(name, 64)[:, 0:64].unsqueeze(1).unsqueeze(1).to_broadcast([64, 2, CT, 64])

            for i in range(2, 4):
                dve.wait_ge(sem("s_tr"), i + 1)
                V.tensor_copy(TOS[i], ps[0:64, 4 + i, :]).then_inc(sem("s_tok_d"), 1)
                dve.drain()
            dve.wait_ge(sem("smat"), 2)
            own(V.tensor_tensor(by_pair(SXT), score_banks(2), mask4("m2T"), ALU.mult))
            dve.wait_ge(sem("s_act"), 1)
            own(V.tensor_tensor(by_head(SXX), by_head(SLR), mask("m2"), ALU.mult))
            V.tensor_tensor(by_head(SXX), by_head(SXX), mask("ident"), ALU.add)
            V.tensor_tensor(by_head(SXT), by_head(SXT), mask("ident"), ALU.add)
            V.tensor_tensor(by_head(SLM), by_head(SLR), mask("m4"), ALU.mult).then_inc(sem("s_inv"), 1)
            dve.drain()
            dve.wait_ge(sem("s_inv"), 1)
            dve.wait_ge(sem("smat"), 5)
            V.tensor_tensor(SXX, SXX, ps[0:64, 7, :], ALU.add)
            V.tensor_tensor(SXT, SXT, ps[0:64, 4, :], ALU.add)
            V.tensor_tensor(by_head(SLM), by_head(SLR), mask("m8"), ALU.mult).then_inc(sem("s_inv"), 1)
            dve.drain()
            dve.wait_ge(sem("s_inv"), 2)
            dve.wait_ge(sem("smat"), 7)
            V.tensor_tensor(SXT, SXT, ps[0:64, 7, :], ALU.add).then_inc(sem("s_dve"), 1)
            dve.drain()
            for i, (out, m) in enumerate(((SMK, "SU8"), (SNB, "IU8"), (SNK, "IU8"))):
                dve.wait_ge(sem("smat"), 8 + i)
                V.tensor_tensor(by_pair(out), score_banks(2 * i), mask4(m), ALU.mult).then_inc(sem("s_dve"), 1)
                dve.drain()
            dve.wait_ge(sem("smat"), 12)
            V.tensor_copy(SXK, ps[:, 5, 0:256]).then_inc(sem("s_dve"), 1)
            dve.drain()
            dve.wait_ge(sem("smat"), 15)
            dve.wait_ge(sem("s_act"), 5)
            V.tensor_tensor(SUU, SW1, ps[0:64, 7, :], ALU.add).then_inc(sem("s_dve"), 1)
            dve.drain()
            dve.wait_ge(sem("s_dve"), 6)
            dve.wait_ge(sem("smat"), 16)
            dve.wait_ge(sem("s_tok_d"), 2)
            dve.wait_ge(sem("o_new"), 1)
            V.tensor_tensor(o_rw[:, :, SEQ:NT], o_rw[:, :, SEQ:NT], ps[:, 0, 0:256].rearrange("p (c n) -> p c n", c=CT), ALU.add)\
                .then_inc(sem("o_sample"), 1)
            dve.drain()
            seq = K("seq", 64).unsqueeze(2).to_broadcast([64, 8, 64])
            for ct in range(CT):
                for h in range(2):
                    if ct:
                        dve.wait_ge(sem("s_dstate"), 2 * ct + h - 1)
                    for a, src in ((0, SUU), (1, TOS[3])):
                        ins = V.tensor_tensor(by_head(SPREAD[h][a]), src[:, hc(ct, h)].unsqueeze(1).to_broadcast([64, 8, 64]),
                                              seq, ALU.mult)
                    ins.then_inc(sem("s_spread"), 1)
                    dve.drain()
                if ct:
                    new_state(dve, own, ct - 1)
            new_state(dve, own, CT - 1)

        def new_state(dve, own, ct):
            V = nc.vector
            dve.wait_ge(sem("s_dstate"), 2 * ct + 2)
            own(V.tensor_tensor(SST[:, ct, :], SST[:, ct, :], ps[:, 5 + ct % 2, :], ALU.add))
            s3 = SST[:, ct, :].rearrange("p (b n) -> p b n", b=DB)
            V.tensor_tensor(s3, s3, SVP[:, ct, :].unsqueeze(2).to_broadcast([128, DB, DH]), ALU.mult).then_inc(sem("s_new"), 1)
            dve.drain()

        FO, FS, FX, FY, FT = EP, EM, CC, CX, TT

        def rwout_pe(pe):
            for ct in range(CT):
                if ct == 0:
                    pe.wait_ge(sem("o_sample"), 1)
                    pe.wait_ge(sem("s_new"), CT)
                else:
                    pe.wait_ge(sem("rw_out"), ct)
                for c in range(2):
                    last = nc.tensor.matmul(ps[:, 4 + c, 0:HC], K("bones"), o_rw[:, ct, c * HC:(c + 1) * HC], start=True, stop=True)
                last.then_inc(sem("ln_mean"), 1)
                pe.wait_ge(sem("ln_sq"), ct + 1)
                for c in range(2):
                    last = nc.tensor.matmul(ps[:, 6 + c, 0:HC], K("bones"), FS[:, c * HC:(c + 1) * HC], start=True, stop=True)
                last.then_inc(sem("ln_var"), 1)
                for c in range(2):
                    last = nc.tensor.matmul(ps[:, 4 + c, 0:HC], GL[:, 128 * ct:128 * ct + 128], UG[:, c * HC:(c + 1) * HC],
                                            start=True, stop=True)
                last.then_inc(sem("gate_lora"), 1)

        def rwout_act(act, own):
            for ct in range(CT):
                act.wait_ge(sem("ln_centred"), ct + 1)
                nc.scalar.activation(FS[:, :], FO[:, :], ACT.Square).then_inc(sem("ln_sq"), 1)
                act.drain()
                act.wait_ge(sem("ln_var"), ct + 1)
                rsqrt_act(own, bank2(6), FX[:, :], FY[:, :], 1.0 / DH, 2)

        def rwout_dve(dve, own):
            V = nc.vector
            for ct in range(CT):
                dve.wait_ge(sem("ln_mean"), ct + 1)
                V.scalar_tensor_tensor(two(FO[:, :]), bank2(4), -1.0 / DH, two(o_rw[:, ct, :]), ALU.mult, ALU.add)\
                    .then_inc(sem("ln_centred"), 1)
                dve.drain()
                rsqrt_dve(own, dve, RS_FIN + ct + 1, FX[:, :], FY[:, :], FT[:, :])
                own(V.tensor_tensor(FT[:, :], FO[:, :], FY[:, :], ALU.mult))
                own(V.tensor_scalar(FT[:, :], FT[:, :], P1("lng", ct), P1("lnb", ct), ALU.mult, ALU.add))
                own(V.tensor_tensor(FT[:, :], FT[:, :], BN[:, ct, :], ALU.add))
                dve.wait_ge(sem("gate_lora"), ct + 1)
                V.tensor_tensor(two(o_rw[:, ct, :]), two(FT[:, :]), bank2(4), ALU.mult).then_inc(sem("rw_out"), 1)
                dve.drain()

        def at_units(cc, c2):
            return [(P_ATT + 9 * cc + (9 * c2 + n) // 2, (9 * c2 + n) % 2, n) for n in range(9)]

        ITS = [(h, n) for h in range(2) for n in range(4)]

        def widths(n):
            return (128 if n == 0 else 256, 128 * (n + 1), 128 * (n + 1))

        def key_tiles(n):
            return ([(0, k) for k in range(max(0, n - 1), n + 1)] + [(g, k) for g in (1, 2) for k in range(n + 1)])

        def batches(tiles):
            return [tiles[i:i + 4] for i in range(0, len(tiles), 4)]

        NBAT = [len(batches(key_tiles(n))) for _, n in ITS]
        PER = sum(NBAT) + 3
        SBANK = ((4, 5, 6), (1, 2, 3))
        TBANK = (0, 7)
        STILES = ([(0, 128)] + [(KOFF[1] + 128 * i, 128) for i in range(4)] + [(KOFF[2] + 128 * i, 128) for i in range(4)]
                  + [(128 + 64 * g, 64) for g in range(3)])

        def q_index(n):
            return 2 * (n // 3) + n % 3

        def att_pe(pe):
            with pe.Fori(0, 2) as cc:
                for c2 in range(2):
                    hp = 2 * cc + c2
                    us = at_units(cc, c2)

                    def post(n):
                        g, kind = n // 3, n % 3
                        if kind < 2:
                            i = q_index(n)
                            pe.wait_ge(sem("qk_sq"), 6 * hp + i + 1)
                            pe.wait_ge(sem("rsqrt_guess"), RS_ATT + 6 * hp + i)
                            if n == 0:
                                pe.wait_ge(sem("so_evac"), hp)
                            for c in range(2):
                                last = nc.tensor.matmul(ps[:, 4 + c, 0:HC], K("bones"), asq[:, c * HC:(c + 1) * HC],
                                                        start=True, stop=True)
                            last.then_inc(sem("qk_norm"), 1)
                        else:
                            pe.wait_ge(evac[us[n][1]], us[n][0] + 1)
                            pe.wait_ge(sem("v_evac"), 3 * hp + g)
                            for T in range(4):
                                nc.tensor.transpose(ps[:, 6, 128 * T:128 * T + 128], QKV[:, g, 2, 128 * T:128 * T + 128], K("ident"))
                            nc.tensor.transpose(ps[0:64, 7, 0:128], QKV[:, g, 2, SEQ:NT], K("ident")).then_inc(sem("v_tr"), 1)

                    for P, q, n in us:
                        unit(pe, P, q)
                        if n:
                            post(n - 1)
                    post(8)
                    pe.wait_ge(sem("qk_applied"), 6 * hp + 6)
                    pe.wait_ge(sem("v_evac"), 3 * hp + 3)
                    for q in range(2):
                        last_u = [u for u in us if u[1] == q][-1]
                        pe.wait_ge(evac[q], last_u[0] + 1)

                    def scores(it):
                        h, n = ITS[it]
                        r = rows_of(h)
                        if it >= 2:
                            pe.wait_ge(sem("pv_evac"), 8 * hp + it - 1)
                        for g, w in enumerate(widths(n)):
                            k0 = 128 * (n + 1) - w
                            last = nc.tensor.matmul(ps[:, SBANK[it % 2][g], 0:w], QKV[r, g, 0, 128 * n:128 * n + 128],
                                                    QKV[r, g, 1, k0:k0 + w], start=True, stop=True)
                        last.then_inc(sem("s_scores"), 1)

                    bat = 0
                    scores(0)
                    for it, (h, n) in enumerate(ITS):
                        if it + 1 < len(ITS):
                            scores(it + 1)
                        pe.wait_ge(sem("p_exp"), 9 * hp + it + 1)
                        c = 0
                        groups = batches(key_tiles(n))
                        first = bat
                        for tiles in groups:
                            pe.wait_ge(sem("pt_evac"), PER * hp + bat - 1) if bat >= 2 else None
                            for i, _ in enumerate(tiles):
                                last = nc.tensor.transpose(ps[:, TBANK[bat % 2], 128 * i:128 * i + 128], SB[it % 2][:, c:c + 128], K("ident"))
                                c += 128
                            last.then_inc(sem("pt_done"), 1)
                            bat += 1
                        o = ps[:, SBANK[it % 2][0], 256:320]
                        kt = 0
                        for i, tiles in enumerate(groups):
                            pe.wait_ge(sem("pt_evac"), PER * hp + first + i + 1)
                            for g, k in tiles:
                                last = nc.tensor.matmul(o, PT[:, kt, :], VT[:, g, k, 64 * h:64 * h + 64], start=(kt == 0),
                                                        stop=(kt == len(key_tiles(n)) - 1))
                                kt += 1
                        last.then_inc(sem("pv_done"), 1)
                    pe.wait_ge(sem("pv_evac"), 8 * hp + 8)
                    for n in range(4):
                        last = nc.tensor.transpose(ps[:, 5, 128 * n:128 * n + 128], OA[:, n, :], K("ident"))
                    last.then_inc(sem("oa_tr"), 1)
                    pe.wait_ge(sem("q_spread"), hp + 1)
                    for g in range(3):
                        nc.tensor.matmul(ps[:, 1, 128 + 64 * g:192 + 64 * g], QA[:, g, :], QKV[:, g, 1, SEQ:NT], start=(g == 0),
                                         stop=False, skip_group_check=True)
                    for b in range(DB):
                        pe.wait_ge(sem("kc_loaded%d" % (b % 2)), 16 * (4 * hp + b // 2 + 1))
                        o, k0 = slice(32 * (b // 2), 32 * (b // 2) + 32), 0
                        for g in range(3):
                            last = nc.tensor.matmul(ps[o, 1 + g, 0:CK[g]], QB[:, g, b, :], KC[b % 2][:, k0:k0 + CK[g]],
                                                    start=(g > 0 and b % 2 == 0), stop=(b % 2 == 1), skip_group_check=True)
                            k0 += CK[g]
                        last.then_inc(sem("kc_used"), 1)
                    pe.wait_ge(sem("sp_ready"), hp + 1)
                    for tl in range(3):
                        pe.wait_ge(sem("pt_evac"), PER * hp + bat - 1)
                        for i in range(4):
                            c, w = STILES[4 * tl + i]
                            last = nc.tensor.transpose(ps[0:w, TBANK[bat % 2], 128 * i:128 * i + 128], SB[0][:, c:c + w], K("ident"))
                        last.then_inc(sem("pt_done"), 1)
                        bat += 1
                    assert bat == PER
                    pe.wait_ge(sem("pt_evac"), PER * hp + PER)
                    pe.wait_ge(sem("o_at_evac"), hp + 1)
                    for b in range(DB):
                        pe.wait_ge(sem("vc_loaded%d" % (b % 2)), 16 * (4 * hp + b // 2 + 1))
                        c = slice(16 * b, 16 * b + 16)
                        for k in range(9):
                            last = nc.tensor.matmul(ps[:, 4, c], VC[b % 2][:, k, :], PT[:, k, c], start=(k == 0), stop=False)
                        last.then_inc(sem("vc_used"), 1)
                        for g in range(3):
                            last = nc.tensor.matmul(ps[:, 4, c], VS[:, g, :], PT[0:64, 9 + g, c], start=False, stop=(g == 2))
                    last.then_inc(sem("so_done"), 1)

        def att_act(act, own):
            with act.Fori(0, 2) as cc:
                own.enter(cc, 2 * (2 * 6))
                for c2 in range(2):
                    hp = 2 * cc + c2

                    def guess(n):
                        act.wait_ge(sem("qk_norm"), 6 * hp + q_index(n) + 1)
                        act.wait_ge(sem("qk_applied"), 6 * hp + q_index(n))
                        rsqrt_act(own, bank2(4), arx[:, :], ary[:, :], 1.0 / DH, 0)

                    act.wait_ge(sem("kv_stored"), 16 * hp)
                    for P, q, n in at_units(cc, c2):
                        g, kind = n // 3, n % 3
                        act.wait_ge(unit_done, B5(P, q))
                        if kind < 2:
                            act.wait_ge(sem("qk_norm"), 6 * hp + q_index(n))
                            nc.scalar.activation(two(asq[:, :]), bank2(2 * q), ACT.Square).then_inc(sem("qk_sq"), 1)
                            act.drain()
                        nc.scalar.activation(two(QKV[:, g, kind, :]), bank2(2 * q), ACT.Copy).then_inc(evac[q], 1)
                        act.drain()
                        split_hi(act, P + 1, q, W8)
                        if n and (n - 1) % 3 < 2:
                            guess(n - 1)
                    act.wait_ge(sem("qk_applied"), 6 * hp + 6)
                    act.wait_ge(evac[us_last(cc, c2)[1]], us_last(cc, c2)[0] + 1)
                    act.dma_start(t["kvT"][hp], QKV[:, :, 1:3, :]).then_inc(sem("kv_stored"), 16)
                    bat = 0
                    for it, (h, n) in enumerate(ITS):
                        w = sum(widths(n))
                        act.wait_ge(sem("p_max"), 9 * hp + it + 1)
                        nc.scalar.activation(SB[it % 2][:, 0:w], SB[it % 2][:, 0:w], ACT.Exp, bias=mx[:, it % 2],
                                             accum_out=ls[:, it % 2]).then_inc(sem("p_exp"), 1)
                        act.drain()
                        c = 0
                        for tiles in batches(key_tiles(n)):
                            act.wait_ge(sem("pt_done"), PER * hp + bat + 1)
                            m = len(tiles)
                            nc.scalar.activation(PT[:, c:c + m, :].rearrange("p k n -> p (k n)"), ps[:, TBANK[bat % 2], 0:128 * m],
                                                 ACT.Copy).then_inc(sem("pt_evac"), 1)
                            act.drain()
                            c += m
                            bat += 1
                    act.wait_ge(sem("oa_tr"), hp + 1)
                    nc.scalar.activation(o_at[:, hp, 0:SEQ], ps[:, 5, :], ACT.Copy).then_inc(sem("o_at_evac"), 1)
                    act.drain()
                    act.wait_ge(sem("p_max"), 9 * hp + 9)
                    nc.scalar.activation(SB[0][:, :], SB[0][:, :], ACT.Exp, bias=mx[:, 0], accum_out=ls[:, 0]).then_inc(sem("p_exp"), 1)
                    act.drain()
                    for tl in range(3):
                        act.wait_ge(sem("pt_done"), PER * hp + bat + 1)
                        full = 4 if tl < 2 else 1
                        b = TBANK[bat % 2]
                        ins = nc.scalar.activation(PT[:, 4 * tl:4 * tl + full, :].rearrange("p k n -> p (k n)"), ps[:, b, 0:128 * full], ACT.Copy)
                        if full == 1:
                            ins = nc.scalar.activation(PT[0:64, 9:12, :].rearrange("p k n -> p (k n)"), ps[0:64, b, 128:512], ACT.Copy)
                        ins.then_inc(sem("pt_evac"), 1)
                        act.drain()
                        bat += 1
                own.leave(2)

        def us_last(cc, c2):
            return at_units(cc, c2)[-1]

        def att_dve(dve, own):
            V = nc.vector
            V.memset(QB[:, :, :, :].rearrange("p g b n -> p (g b n)"), 0.0)
            own(V.memset(QA[:, :, :].rearrange("p g n -> p (g n)"), 0.0))
            own(V.tensor_scalar(par[:, COLS["qg"]:COLS["qg"] + 3, 0], par[:, COLS["qg"]:COLS["qg"] + 3, 0], DH ** -0.5, None, ALU.mult))
            dve.wait_ge(sem("mask_loaded"), 16)
            with dve.Fori(0, 2) as cc:
                own.enter(cc, 2 * (3 * 6 + 2 * 9 + 8 + 1))
                for c2 in range(2):
                    hp = 2 * cc + c2
                    us = at_units(cc, c2)

                    def apply(n):
                        g, kind = n // 3, n % 3
                        rsqrt_dve(own, dve, RS_ATT + 6 * hp + q_index(n) + 1, arx[:, :], ary[:, :], art[:, :])
                        a = QKV[:, g, kind, :]
                        V.scalar_tensor_tensor(a, a, P1("qg" if kind == 0 else "kg", g), ary[:, :], ALU.mult, ALU.mult)\
                            .then_inc(sem("qk_applied"), 1)
                        dve.drain()

                    def v_out(g):
                        dve.wait_ge(sem("v_tr"), 3 * hp + g + 1)
                        V.tensor_copy(VT[:, g].rearrange("p t n -> p (t n)"), ps[:, 6, :])
                        V.tensor_copy(VS[:, g, :], ps[0:64, 7, 0:128]).then_inc(sem("v_evac"), 1)
                        dve.drain()

                    for n in range(9):
                        if n % 3 < 2:
                            apply(n)
                        else:
                            v_out(n // 3)
                    dve.wait_ge(sem("qk_applied"), 6 * hp + 6)
                    for h in range(2):
                        r = rows_of(h)
                        for g in range(3):
                            src = QKV[r, g, 0, SEQ:NT].rearrange("p (b t) -> p b t", t=DS)
                            for e in range(2):
                                V.tensor_copy(QB[r, g, e:DB:2, 16 * e + 8 * h:16 * e + 8 * h + 8], src[:, e:DB:2, :])
                            ins = V.tensor_copy(QA[r, g, :].rearrange("p (b n) -> p b n", n=16)[:, :, 8 * h:8 * h + 8], src)
                    ins.then_inc(sem("q_spread"), 1)
                    dve.drain()

                    def row_max(i, w):
                        own(V.reduce_max(mx[:, i], SB[i][:, 0:w], AX.X))
                        V.tensor_scalar(mx[:, i], mx[:, i], -1.0, None, ALU.mult).then_inc(sem("p_max"), 1)
                        dve.drain()

                    def biased(it):
                        h, n = ITS[it]
                        dve.wait_ge(sem("s_scores"), 8 * hp + it + 1)
                        if it >= 2:
                            dve.wait_ge(sem("pv_done"), 8 * hp + it - 1)
                        c = 0
                        for g, w in enumerate(widths(n)):
                            m0 = (256, 768, 1280)[g] - w
                            ins = V.scalar_tensor_tensor(SB[it % 2][:, c:c + w], MSK[:, m0:m0 + w], P1("slp", 2 * hp + h),
                                                         ps[:, SBANK[it % 2][g], 0:w], ALU.mult, ALU.add)
                            c += w
                        own(ins)
                        row_max(it % 2, c)

                    biased(0)
                    for it, (h, n) in enumerate(ITS):
                        if it + 1 < len(ITS):
                            biased(it + 1)
                        dve.wait_ge(sem("p_exp"), 9 * hp + it + 1)
                        own(V.reciprocal(ls[:, it % 2], ls[:, it % 2]))
                        dve.wait_ge(sem("pv_done"), 8 * hp + it + 1)
                        V.tensor_scalar(OA[:, n, 64 * h:64 * h + 64], ps[:, SBANK[it % 2][0], 256:320], ls[:, it % 2], None, ALU.mult)\
                            .then_inc(sem("pv_evac"), 1)
                        dve.drain()
                    dve.wait_ge(sem("kc_used"), 8 * hp + 8)
                    for i, (c, w) in enumerate(((0, 320), (320, 512), (832, 512))):
                        ins = V.scalar_tensor_tensor(SB[0][:, c:c + w], MSK[:, 1280 + c:1280 + c + w], P1("sls", hp), ps[:, 1 + i, 0:w],
                                                     ALU.mult, ALU.add)
                    own(ins)
                    row_max(0, NKEY)
                    dve.wait_ge(sem("p_exp"), 9 * hp + 9)
                    own(V.reciprocal(ls[:, 0], ls[:, 0]))
                    V.tensor_scalar(SB[0][:, :], SB[0][:, :], ls[:, 0], None, ALU.mult).then_inc(sem("sp_ready"), 1)
                    dve.drain()
                    dve.wait_ge(sem("so_done"), hp + 1)
                    for h in range(2):
                        r = rows_of(h)
                        ins = V.tensor_copy(o_at[r, hp, SEQ:NT].rearrange("p (b t) -> p b t", t=DS),
                                            ps[r, 4, 0:128].rearrange("p (b n) -> p b n", n=16)[:, :, 8 * h:8 * h + 8])
                    ins.then_inc(sem("so_evac"), 1)
                    dve.drain()
                own.leave(2)

        def mrg_units(jj, c2):
            return [(P_MRG + 3 * jj + (3 * c2 + n) // 2, (3 * c2 + n) % 2) for n in range(3)]

        def merge_pe(pe):
            with pe.Fori(0, 4) as jj:
                for c2 in range(2):
                    j = 2 * jj + c2
                    us = mrg_units(jj, c2)
                    unit(pe, *us[0])
                    unit(pe, *us[1])
                    pe.wait_ge(sem("o_split"), 8)
                    pe.wait_ge(sem("m_ready"), j)
                    unit_wait(pe, *us[2])
                    three_pass(us[2][1], o_hi, o_lo, 0, 4, 4)
                    three_pass(us[2][1], o_hi[:, 4:8], o_lo[:, 4:8], 4, 4, 6, ).then_inc(unit_done, 1)
            pe.wait_ge(sem("m_ready"), KD)
            with pe.Fori(0, 4) as jj:
                for q in range(2):
                    unit(pe, P_OUT + jj, q, m_hi, m_lo)

        def merge_act(act):
            for k in range(8):
                src = o_at[:, k, :] if k < 4 else o_rw[:, k - 4, :]
                nc.scalar.activation(o_hi[:, k, :], src, ACT.Copy).then_inc(sem("o_hi_ready"), 1)
                act.drain()
            with act.Fori(0, 4) as jj:
                for c2 in range(2):
                    j = 2 * jj + c2
                    us = mrg_units(jj, c2)
                    for n, out in ((0, sA), (1, sR)):
                        P, q = us[n]
                        act.wait_ge(unit_done, B5(P, q))
                        act.wait_ge(sem("mrg_ready"), j)
                        nc.scalar.activation(two(out[:, :]), bank2(2 * q), ACT.Sigmoid).then_inc(evac[q], 1)
                        act.drain()
                        split_hi(act, P + 1, q, W8)
                    split_hi(act, us[2][0] + 1, us[2][1], W8)
                    act.wait_ge(sem("mrg_ready"), j + 1)
                    nc.scalar.activation(m_hi[:, j, :], mA[:, :], ACT.Copy).then_inc(sem("m_hi_ready"), 1)
                    act.drain()
            with act.Fori(0, 4) as jj:
                for q in range(2):
                    split_hi(act, P_OUT + jj + 1, q, W8)

        def merge_dve(dve, own):
            V = nc.vector
            for k in range(8):
                src = o_at[:, k, :] if k < 4 else o_rw[:, k - 4, :]
                dve.wait_ge(sem("o_hi_ready"), k + 1)
                V.tensor_tensor(o_lo[:, k, :], src, o_hi[:, k, :].bitcast(F32), ALU.subtract).then_inc(sem("o_split"), 1)
                dve.drain()
            with dve.Fori(0, 4) as jj:
                own.enter(jj, 2)
                for c2 in range(2):
                    j = 2 * jj + c2
                    us = mrg_units(jj, c2)
                    for P, q in us[:2]:
                        dve.wait_ge(evac[q], P + 1)
                    P, q = us[2]
                    dve.wait_ge(unit_done, B5(P, q))
                    own(V.tensor_tensor(two(mA[:, :]), two(sA[:, :]), bank2(4), ALU.mult))
                    V.tensor_tensor(two(sR[:, :]), two(sR[:, :]), bank2(6), ALU.mult).then_inc(evac[q], 1)
                    dve.drain()
                    dve.wait_ge(evac[q], P + 1)
                    V.tensor_tensor(mA[:, :], mA[:, :], sR[:, :], ALU.add).then_inc(sem("mrg_ready"), 1)
                    dve.drain()
                    dve.wait_ge(sem("mrg_ready"), j + 1)
                    dve.wait_ge(sem("m_hi_ready"), j + 1)
                    V.tensor_tensor(m_lo[:, j, :], mA[:, :], m_hi[:, j, :].bitcast(F32), ALU.subtract).then_inc(sem("m_ready"), 1)
                    dve.drain()
                own.leave(4)
            with dve.Fori(0, 4) as jj:
                for q in range(2):
                    P = P_OUT + jj
                    dve.wait_ge(unit_done, 2 * P + q + 1)
                    V.tensor_tensor(two(x[:, 2 * jj + q, :]), two(x[:, 2 * jj + q, :]), bank2(2 * q), ALU.add).then_inc(evac[q], 1)
                    dve.drain()

        block = ctx.enter_context(nc.Block())
        own_act, own_dve = sem("act_own_steps"), sem("dve_own_steps")
        n_cache = 0

        @block.tensor
        def _(pe):
            norm_pe(pe, 0)
            ffn_pe(pe, 0, P_FFN1)
            barrier(pe, 1)
            norm_pe(pe, 1)
            rwkv_pe(pe)
            barrier(pe, 2)
            rwsam_pe(pe)
            rwout_pe(pe)
            barrier(pe, 3)
            att_pe(pe)
            barrier(pe, 4)
            merge_pe(pe)
            barrier(pe, 5)
            norm_pe(pe, 2)
            ffn_pe(pe, 1, P_FFN2)
            barrier(pe, 6)

        @block.scalar
        def _(act):
            own = Own(act, own_act)
            act.dma_start(x[:, :, :], t["xT"]).then_inc(sem("x_loaded"), 16)
            act.dma_start(par[:, :, 0], t["par"]).then_inc(sem("x_loaded"), 16)
            act.dma_start(con[:, :], t["con"]).then_inc(sem("x_loaded"), 16)
            for g in range(3):
                drop = DS if g < 2 else 0
                for b in range(DB):
                    act.dma_start(t["cache_out%d" % g][b], t["cache%d" % g][b, drop:PASTS[g], :]).then_inc(sem("cache_copied"), 16)
            norm_act(act, own, 0)
            for q in range(2):
                split_hi(act, 0, q, W8)
            ffn_act(act, 0, P_FFN1)
            barrier(act, 1)
            norm_act(act, own, 1)
            rwkv_act(act, own)
            barrier(act, 2)
            rwsam_act(act, own)
            rwout_act(act, own)
            act.wait_ge(sem("wkvp_stored"), 16 * CT)
            act.wait_ge(sem("wkvs_stored"), 16 * CT)
            act.wait_ge(sem("shift_stored"), 16)
            barrier(act, 3)
            att_act(act, own)
            act.wait_ge(sem("kv_stored"), 16 * CT)
            barrier(act, 4)
            merge_act(act)
            barrier(act, 5)
            norm_act(act, own, 2)
            ffn_act(act, 1, P_FFN2)
            barrier(act, 6)

        @block.vector
        def _(dve):
            own = Own(dve, own_dve)
            norm_dve(dve, own, 0, "g1")
            ffn_dve(dve, 0, P_FFN1)
            barrier(dve, 1)
            norm_dve(dve, own, 1, "gm")
            rwkv_dve(dve, own)
            barrier(dve, 2)
            rwsam_dve(dve, own)
            rwout_dve(dve, own)
            barrier(dve, 3)
            att_dve(dve, own)
            barrier(dve, 4)
            merge_dve(dve, own)
            barrier(dve, 5)
            norm_dve(dve, own, 2, "g2")
            ffn_dve(dve, 1, P_FFN2)
            barrier(dve, 6)

        @block.gpsimd
        def _(pool):
            ffn_pool(pool, P_FFN1)
            with pool.Fori(P_RW, P_FFN2) as P:
                for q in range(2):
                    split_lo(pool, P, q, W8)
            ffn_pool(pool, P_FFN2)

        @block.sync
        def _(sp):
            ffn_sp(sp, P_FFN1, 0, 0)

            def mid_pair(P):
                for q in range(2):
                    load_unit(sp, P, q, t["w8"][44 + 2 * (P - P_RW) + q], W8)

            mid_pair(P_RW)
            mid_pair(P_RW + 1)
            sp.wait_ge(sem("h_ready"), 16)
            sp.dma_start(SH0[:, :, :], t["shift0"]).then_inc(sem("rw_loaded"), 16)
            sp.dma_start(GL[:, :], t["g_up"]).then_inc(sem("rw_loaded"), 16)
            with sp.Fori(0, 2) as cc:
                sp.wait_ge(sem("lora_done"), 4 * cc)
                for c2 in range(2):
                    sp.dma_start(LO[c2][:, :], t["lora"][2 * cc + c2]).then_inc(sem("lora_w%d" % c2), 16)
                for i in range(3):
                    mid_pair(P_RW + 2 + 3 * cc + i)
            mid_pair(P_RW + 8)
            sp.wait_ge(sem("phase2_over"), 3)
            sp.dma_start(SST, t["state"]).then_inc(sem("s_states"), 16)
            sp.wait_ge(sem("phase3_over"), 3)
            sp.dma_start(MSK[:, :], t["masks"]).then_inc(sem("mask_loaded"), 16)
            with sp.Fori(0, 2) as cc:
                for c2 in range(2):
                    hp = 2 * cc + c2
                    for i in range(9):
                        k = 9 * c2 + i
                        load_unit(sp, P_RW + 9 + 9 * cc + k // 2, k % 2, t["w8"][44 + 18 + 18 * cc + k], W8)

                    def k_load(b):
                        sp.wait_ge(sem("kc_used"), 8 * hp + b - 1) if b >= 2 else sp.wait_ge(sem("kc_used"), 8 * hp)
                        sp.dma_start(KC[b % 2][:, :], t["kc"][hp, b]).then_inc(sem("kc_loaded%d" % (b % 2)), 16)

                    def v_load(b):
                        sp.wait_ge(sem("vc_used"), 8 * hp + b - 1) if b >= 2 else sp.wait_ge(sem("vc_used"), 8 * hp)
                        sp.dma_start(VC[b % 2][:, :, :], t["vc"][hp, b]).then_inc(sem("vc_loaded%d" % (b % 2)), 16)

                    for b in range(2):
                        k_load(b)
                        v_load(b)
                    for b in range(2, DB):
                        k_load(b)
                    for b in range(2, DB):
                        v_load(b)
            with sp.Fori(P_RW + 27, P_FFN2) as P:
                mid_pair(P)
            ffn_sp(sp, P_FFN2, 126, 16)
            for q in range(2):
                load_unit(sp, N_PAIR, q, t["w8"][170 + q], W8)
            sp.wait_ge(sem("phase6_over"), 3)
            sp.dma_start(t["yT"], x[:, :, :]).then_inc(sem("y_stored"), 16)
            sp.wait_ge(sem("y_stored"), 16)
            sp.wait_ge(sem("cache_copied"), 16 * 24)
            sp.wait_ge(sem("kv_stored"), 16 * CT)
            sp.wait_ge(sem("wkvp_stored"), 16 * CT)
            sp.wait_ge(sem("wkvs_stored"), 16 * CT)
            sp.wait_ge(sem("shift_stored"), 16)


def tiles8(w, cols):
    k = w.shape[0] // 128
    return w[:, cols:cols + 128].reshape(k, 128, 128).transpose(1, 0, 2).reshape(128, k * 128)


def kernel(**inputs):
    import concourse.bacc as bacc
    from concourse.bass_utils import run_bass_kernel_spmd

    a = {k: np.asarray(v) for k, v in inputs.items()}
    f32 = np.float32
    A_COLS, S_COLS = 3 * 3 * 512, 1792
    w_in = a["w_in"][0]
    zero = np.zeros((128, W8), f32)

    def ffn8(f):
        g, u = a["ffn%d_w_gate" % f][0], a["ffn%d_w_up" % f][0]
        return [tiles8(m, 128 * j) for j in range(NF) for m in (g, u)]

    def ffn11(f):
        d = a["ffn%d_w_down" % f][0]
        return [tiles8(d[HALF * 128 * hf:HALF * 128 * (hf + 1)], 128 * j) for hf in range(2) for j in range(KD)]

    mids = [tiles8(w_in, A_COLS + 128 * i) for i in (12, 13)]
    mids += [tiles8(w_in, A_COLS + 128 * (4 * n + ct)) for ct in range(CT) for n in range(3)]
    mids += [tiles8(w_in, 1536 * g + 512 * kind + 128 * hp) for hp in range(CT) for g in range(3) for kind in range(3)]
    wa, wr, wo = a["w_branch_attn"][0], a["w_branch_rwkv"][0], a["w_out"][0]
    for j in range(KD):
        mids.append(tiles8(w_in, A_COLS + S_COLS + 128 * j))
        mids.append(tiles8(w_in, A_COLS + S_COLS + D + 128 * j))
        mids.append(np.concatenate([tiles8(wa, 128 * j), tiles8(wr, 128 * j)], axis=1))
    mids += [tiles8(wo, 128 * j) for j in range(KD)]
    w8 = np.stack(ffn8(1) + mids + ffn8(2) + [zero, zero])
    w11 = np.stack(ffn11(1) + ffn11(2))

    def cols(v, n):
        return v.reshape(n, 128).T

    slopes = (2.0 ** (-np.arange(1, 9, dtype=np.float64))).astype(f32)
    par = np.concatenate([
        cols(a["ffn1_norm"][0], 8), cols(a["mix_norm"][0], 8), cols(a["ffn2_norm"][0], 8), cols(a["rwkv_mu"][0], 14),
        cols(a["rwkv_w0"][0], 4), cols(a["rwkv_a0"][0], 4), cols(a["rwkv_k_k"][0], 4), cols(a["rwkv_k_a"][0], 4),
        cols(a["rwkv_r_k"][0].reshape(-1), 4), cols(a["rwkv_ln_gain"][0], 4), cols(a["rwkv_ln_bias"][0], 4),
        np.concatenate([a["attn_q_norm"][0]] * 2, axis=1).T, np.concatenate([a["attn_k_norm"][0]] * 2, axis=1).T,
        np.broadcast_to(slopes, (128, 8)),
        slopes.reshape(4, 2)[:, (np.arange(128) // 8) % 2].T,
        np.broadcast_to(np.array([RMS_EPS, KK_EPS, LN_EPS], f32), (128, 3))], axis=1)
    con, masks = constants()
    xs = np.concatenate([a["x_prompt"][0], a["x_sample"].reshape(NS, D)])
    caches = [a["cache_kv_w%d" % w][0] for w, _ in GROUPS]
    kcs, vcs = [], []
    for g in range(3):
        c = caches[g][:, sample_positions(g)]
        kcs.append(c[:, :, 0].reshape(DB, CK[g], CT, 128).transpose(2, 0, 3, 1))
        vcs.append(c[:, :, 1].reshape(DB, CK[g] // 128, 128, CT, 128).transpose(3, 0, 2, 1, 4))
    arrays = {
        "xT": xs.T.reshape(KD, 128, NT).transpose(1, 0, 2), "par": par, "con": con, "masks": masks, "w8": w8, "w11": w11,
        "shift0": a["state_shift"][0].T.reshape(SHT, 128, DB).transpose(1, 0, 2), "g_up": a["rwkv_g_lora_up"][0],
        "lora": np.concatenate([a["rwkv_w_lora_up"][0], a["rwkv_a_lora_up"][0]]).reshape(128, CT, 128).transpose(1, 0, 2),
        "state": a["state_wkv"][0].reshape(DB, CT, 2, DH, DH).transpose(2, 4, 1, 0, 3).reshape(128, CT, 512),
        "kc": np.concatenate(kcs, axis=3), "vc": np.concatenate(vcs, axis=3),
    }
    for g in range(3):
        arrays["cache%d" % g] = caches[g].reshape(DB, PASTS[g], 1024)
    arrays = {k: np.ascontiguousarray(v, dtype=f32) for k, v in arrays.items()}
    outs = {"yT": (128, KD, NT), "kvT": (CT, 128, 3, 2, NT), "wkv_p": (CT, 128, DH), "wkv_s": (CT, 128, 512), "shift": (128, SHT, 9)}
    for g in range(3):
        outs["cache_out%d" % g] = (DB, PASTS[g] - (DS if g < 2 else 0), 1024)
    nc = bacc.Bacc("TRN2", target_bir_lowering=False, num_devices=1)
    t = {k: nc.dram_tensor("in_" + k, v.shape, F32, kind="ExternalInput").ap() for k, v in arrays.items()}
    t.update({k: nc.dram_tensor(k, s, F32, kind="ExternalOutput").ap() for k, s in outs.items()})
    build(nc, t)
    r = run_bass_kernel_spmd(nc, [{"in_" + k: v for k, v in arrays.items()}], core_ids=[0]).results[0]

    y = r["yT"].transpose(2, 1, 0).reshape(NT, D)
    kv = r["kvT"].reshape(CT, 2, DH, 3, 2, NT).transpose(3, 5, 4, 0, 1, 2).reshape(3, NT, 2, 8, DH)
    kv_p = [kv[g, max(0, SEQ - GROUPS[g][0]):SEQ][None, None] for g in range(3)]
    kv_s = [np.concatenate([r["cache_out%d" % g].reshape(DB, -1, 2, 8, DH), kv[g, SEQ:].reshape(DB, DS, 2, 8, DH)], axis=1)[None]
            for g in range(3)]
    wkv_p = r["wkv_p"].reshape(CT, 2, DH, DH).transpose(0, 1, 3, 2).reshape(1, 1, 8, DH, DH)
    wkv_s = r["wkv_s"].reshape(CT, 2, DH, DB, DH).transpose(3, 0, 1, 4, 2).reshape(1, DB, 8, DH, DH)
    sh = r["shift"].transpose(2, 1, 0).reshape(9, SHT * 128)
    return (y[:SEQ][None], y[SEQ:].reshape(DB, DS, D), *kv_p, wkv_p, sh[None, :1], *kv_s, wkv_s, sh[None, 1:])
```

```python
from contextlib import ExitStack

import numpy as np
import concourse.bass as bass
from concourse import mybir

F32 = mybir.dt.float32
F32R = mybir.dt.float32r
ALU = mybir.AluOpType
ACT = mybir.ActivationFunctionType
AX = mybir.AxisListType

D, FF = 1024, 2816
SEQ, DB, DS = 512, 8, 8
NS = DB * DS
NT = SEQ + NS
HC = NT // 2
KD = D // 128
NF = FF // 128
HALF = NF // 2
CT = 4
DH = 64
SHT = 14
GROUPS = ((128, 1), (512, 4), (2048, 16))
PASTS = (128, 512, 1024)
RMS_EPS, KK_EPS, LN_EPS = 1e-6, 1e-12, 64e-5
C0 = float(np.exp(-0.5))
CH = 64
NCH = SEQ // CH
NEG = -3.0e37
CK = (128, 512, 512)
KOFF = (0, 320, 832)
NKEY = 1344

W8, W11 = KD * 128, HALF * 128
P_FFN1, P_RW, P_CT, P_ATT, P_MRG, P_OUT, P_FFN2 = 0, 30, 31, 45, 63, 67, 71
N_PAIR = 101

COLS = {}
_n = 0
for _name, _w in (("g1", 8), ("gm", 8), ("g2", 8), ("mu", 14), ("w0", 4), ("a0", 4), ("kk", 4), ("ka", 4), ("rk", 4),
                  ("lng", 4), ("lnb", 4), ("qg", 3), ("kg", 3), ("slp", 8), ("sls", 4), ("eps", 3)):
    COLS[_name] = _n
    _n += _w
NPAR = _n

KCOL = {}
_n = 0
for _name, _w in (("ident", 128), ("ones", 128), ("bones", 128), ("m2T", 128), ("m2", 128), ("m4", 128), ("m8", 128),
                  ("m16", 128), ("m32", 128), ("m64", 128), ("SU", 128), ("IU", 128), ("SU8", 64), ("IU8", 64),
                  ("seq", 8), ("reset", NT)):
    KCOL[_name] = (_n, _w)
    _n += _w
NCONST = _n
CFIRST = 3 * 128
XL = KD // 2
PIECE = (15, 18, 16)
N_PIECE = 8 + 28 + 64
QKV_ORDER = ((0, 0), (0, 1), (1, 0), (1, 1), (0, 2), (2, 0), (2, 1), (1, 2), (2, 2))
WARM = 3
FILL = {"norm": 5, "tokens": (10, 1, 0, 0), "bonus": 0, "level": (0, 0, 0, 0, 0), "mv": 2, "xk": 2, "chunk": (1, 1, 1, 1, 2, 2, 2, 2)}
LEVELS = ("m4", "m8", "m16", "m32", "m64")
NMASK = 256 + 512 + 512 + NKEY


def constants():
    c = np.zeros((128, NCONST), np.float32)

    def put(name, a):
        o, w = KCOL[name]
        c[:a.shape[0], o:o + w] = a

    r = np.arange(128)
    t, s = r[:, None], r[None, :]
    put("ident", np.eye(128))
    put("ones", np.ones((128, 128)))
    put("bones", (t // 64 == s // 64))
    for b in (2, 4, 8, 16, 32, 64):
        m = (t // b == s // b) & (t % b >= b // 2) & (s % b < b // 2)
        put("m%d" % b, m)
        if b == 2:
            put("m2T", m.T)
    put("SU", (t // CH == s // CH) & (t < s))
    put("IU", (t // CH == s // CH) & (t <= s))
    t, s = t[:64], s[:, :64]
    put("SU8", (t // DS == s // DS) & (t < s))
    put("IU8", (t // DS == s // DS) & (t <= s))
    put("seq", (np.arange(64)[:, None] // DS == np.arange(8)[None, :]))
    reset = np.ones(NT)
    reset[0:SEQ:CH] = 0
    reset[SEQ::DS] = 0
    put("reset", np.broadcast_to(reset, (128, NT)))

    m = np.zeros((128, NMASK), np.float32)
    q = np.arange(128)[:, None]

    def negdist(dist, ok):
        return np.where(ok, -dist, NEG)

    k = np.arange(256)[None, :]
    d = 128 + q - k
    m[:, 0:256] = negdist(d, (d >= 0) & (d <= 128))
    k = np.arange(512)[None, :] - 384
    d = q - k
    for g, o in ((1, 256), (2, 768)):
        m[:, o:o + 512] = negdist(d, (d >= 0) & (d % GROUPS[g][1] == 0) & (d <= GROUPS[g][0]))
    row = np.arange(128)
    b, tt = (row // 16)[:, None], (row % 8)[:, None]
    o = 1280
    for g in range(3):
        p = sample_positions(g)[None, :]
        d = PASTS[g] + tt - p
        m[:, o + KOFF[g]:o + KOFF[g] + CK[g]] = negdist(d, (d % GROUPS[g][1] == 0) & (d <= GROUPS[g][0]))
        kb, kt = (np.arange(64) // 8)[None, :], (np.arange(64) % 8)[None, :]
        d = tt - kt
        m[:, o + 128 + 64 * g:o + 192 + 64 * g] = negdist(d, (kb == b) & (d >= 0) & (d % GROUPS[g][1] == 0))
    return c, m


def sample_positions(g):
    p = np.arange(PASTS[g])
    return p if g < 2 else p[p % 16 < DS]


class Own:

    def __init__(self, eng, sem):
        self.eng, self.sem, self.base, self.k = eng, sem, 0, 0

    def __call__(self, ins):
        ins.then_inc(self.sem, 1)
        self.k += 1
        self.eng.wait_ge(self.sem, self.base + self.k)

    def enter(self, i, per):
        self.saved, self.per = self.base + self.k, per
        self.base, self.k = self.saved + i * per, 0

    def leave(self, count):
        assert self.k == self.per, (self.k, self.per)
        self.base, self.k = self.saved + count * self.per, 0


def build(nc, t):
    ctx = ExitStack()
    sems = {}

    def sem(name):
        if name not in sems:
            sems[name] = ctx.enter_context(nc.semaphore(name))
        return sems[name]

    def sb(c, name, shape, dt=F32):
        return c.enter_context(nc.sbuf_tensor(name, shape, dt))

    with ctx:
        x = sb(ctx, "x", [128, KD, NT])
        h_hi, h_lo = sb(ctx, "h_hi", [128, KD, NT], F32R), sb(ctx, "h_lo", [128, KD, NT], F32R)
        w_raw = [sb(ctx, "w_raw%d" % i, [128, W11]) for i in range(2)]
        w_hi = [sb(ctx, "w_hi%d" % i, [128, W11], F32R) for i in range(2)]
        w_lo = [sb(ctx, "w_lo%d" % i, [128, W11], F32R) for i in range(2)]
        par = sb(ctx, "par", [128, NPAR, 1])
        con = sb(ctx, "con", [128, NCONST])
        ps = ctx.enter_context(nc.psum_tensor("ps", [128, 8, 512], F32))

        def K(name, rows=128):
            o, w = KCOL[name]
            return con[0:rows, o:o + w]

        def P1(name, i=0):
            return par[:, COLS[name] + i]

        with ExitStack() as c:
            g_hi, g_lo = sb(c, "g_hi", [128, HALF, NT], F32R), sb(c, "g_lo", [128, HALF, NT], F32R)
            sg, gt = sb(c, "sg", [128, NT]), sb(c, "gt", [128, NT])
            sq_ffn = [sb(c, "sq%d" % i, [128, NT]) for i in range(2)]
        with ExitStack() as c:
            nrx, nry, nrt = (sb(c, n, [128, NT]) for n in ("nrx", "nry", "nrt"))
            hf = [sb(c, "hf%d" % i, [128, NT]) for i in range(2)]
        mid = ExitStack()
        o_rw = sb(mid, "o_rw", [128, CT, NT])
        with ExitStack() as c:
            PR = [sb(c, "praw%d" % i, [128, NT]) for i in range(2)]
            UR, UK = sb(c, "u_r", [128, NT]), sb(c, "u_k", [128, NT])
            UW, UG = sb(c, "u_wa", [128, NT]), sb(c, "u_g", [128, NT])
            SW, AA, CC, CX = (sb(c, n, [128, NT]) for n in ("sw", "aa", "cum", "cumx"))
            EP, EM, TT = (sb(c, n, [128, NT]) for n in ("exp_p", "exp_m", "tmp"))
            FM = sb(c, "fm", [128, 5, NT])
            KA, BH, KH, RH, UV = (FM[:, i] for i in range(5))
            TOK = sb(c, "tok", [128, 4, 4, 128])
            LR, LM, ZZ, XX, XT = ([sb(c, "%s%d" % (n, h), [128, 512]) for h in range(2)]
                                  for n in ("lraw", "lmask", "zz", "xx", "xt"))
            MV, W1 = sb(c, "mv", [128, 4, 128]), sb(c, "w1", [128, 4, 128])
            XK, UU = sb(c, "xk", [128, 512]), sb(c, "uu", [128, 4, 128])
            ST, STP = sb(c, "st", [128, NCH + 1, DH]), sb(c, "stp", [128, DH])
            BN = sb(c, "bonus", [128, CT, NT])
            GS = [sb(c, "gate_out%d" % i, [128, NT]) for i in range(2)]
            LO = [sb(c, "lora%d" % i, [128, 128]) for i in range(2)]
            SV, SVP = sb(c, "sv", [128, CT, 5, NS]), sb(c, "svp", [128, CT, DB])
            SH, SH0 = sb(c, "sh", [128, SHT, 9]), sb(c, "sh0", [128, SHT, DB])
            GL = sb(c, "gl", [128, 512])
        o_at = sb(mid, "o_at", [128, CT, NT])
        with ExitStack() as c:
            QKV = sb(c, "qkv", [128, 3, 3, NT])
            asq, arx, ary, art = (sb(c, n, [128, NT]) for n in ("asq", "arx", "ary", "art"))
            VT = sb(c, "vtok", [128, 3, 4, 128])
            VS = sb(c, "vsam", [64, 3, 128])
            SB = [sb(c, "scores%d" % i, [128, NKEY]) for i in range(2)]
            PT = sb(c, "pt", [128, 12, 128])
            MSK = sb(c, "amask", [128, NMASK])
            QB = sb(c, "qblk", [128, 3, DB, 32])
            QA = sb(c, "qall", [128, 3, 128])
            KC = [sb(c, "kc%d" % i, [128, 1152]) for i in range(2)]
            VC = [sb(c, "vc%d" % i, [128, 9, 128]) for i in range(2)]
            OS = sb(c, "osam", [128, 256])
            mx, ls = sb(c, "mx", [128, 2, 1]), sb(c, "ls", [128, 2, 1])
        with ExitStack() as c:
            o_hi, o_lo = sb(c, "o_hi", [128, 2 * CT, NT], F32R), sb(c, "o_lo", [128, 2 * CT, NT], F32R)
            m_hi, m_lo = sb(c, "m_hi", [128, KD, NT], F32R), sb(c, "m_lo", [128, KD, NT], F32R)
            GI = [sb(c, "gate_in%d" % i, [128, 2, NT]) for i in range(2)]
            sA, sR, mA = (sb(c, n, [128, NT]) for n in ("sig_a", "sig_r", "mrg"))
        mid.close()
        def flat(a):
            return a[:, :, :].rearrange("p t n -> p (t n)")

        SLR, SLM, SZZ, SXX, SXT, SNK, SMK, SNB, SMV, SW1 = (a[0:64, :] for a in (
            LR[0], LM[0], ZZ[0], XX[0], XT[0], LM[1], ZZ[1], LR[1], XX[1], XT[1]))
        SUU = flat(W1)[0:64]
        TOS = [a[0:64, 0:512] for a in (CC, CX, EM, EP)]
        SPREAD = [[a[0:64, 0:512] for a in p] for p in ((UR, UK), (PR[0], PR[1]))]
        SXK, SU0 = XK[:, 0:256], SW[:, 0:256]
        SST = TOK[:, :, :, :].rearrange("p a t n -> p a (t n)")

        unit_done, hi_done, lo_done = sem("unit_done"), sem("hi_done"), sem("lo_done")
        loaded = [sem("w_loaded_even"), sem("w_loaded_odd")]
        evac = [sem("set0_evacuated"), sem("set1_evacuated")]

        def bank2(b):
            return ps[:, b:b + 2, 0:HC]

        def two(a):
            return a.rearrange("p (c n) -> p c n", c=2)

        def load_unit(sp, P, par_, src, words):
            if not (isinstance(P, int) and P == 0):
                sp.wait_ge(lo_done, 2 * P - 1 + par_)
            sp.dma_start(w_raw[par_][:, 0:words], src).then_inc(loaded[par_], 16)

        def split_hi(act, P, par_, words):
            act.wait_ge(loaded[par_], 16 * (P + 1))
            if not (isinstance(P, int) and P == 0):
                act.wait_ge(unit_done, 2 * P - 1 + par_)
            nc.scalar.activation(w_hi[par_][:, 0:words], w_raw[par_][:, 0:words], ACT.Copy).then_inc(hi_done, 1)
            act.drain()

        def split_lo(pool, P, par_, words):
            pool.wait_ge(hi_done, 2 * P + par_ + 1)
            nc.gpsimd.tensor_tensor(w_lo[par_][:, 0:words], w_raw[par_][:, 0:words],
                                    w_hi[par_][:, 0:words].bitcast(F32), ALU.subtract).then_inc(lo_done, 1)

        def unit_wait(pe, P, par_):
            pe.wait_ge(lo_done, 2 * P + par_ + 1)
            if not (isinstance(P, int) and P == 0):
                pe.wait_ge(evac[par_], P)

        def unit_slice(par_, a_hi, a_lo, kw, k, nk, b):
            wk = slice(kw * 128, (kw + 1) * 128)
            for w, a, first, end in ((w_hi, a_hi, True, False), (w_hi, a_lo, False, False), (w_lo, a_hi, False, True)):
                for c in range(2):
                    last = nc.tensor.matmul(ps[:, b + c, 0:HC], w[par_][:, wk], a[:, k, c * HC:(c + 1) * HC],
                                            start=(first and k == 0), stop=(end and k == nk - 1))
            return last

        def three_pass(par_, a_hi, a_lo, k0, nk, b, ready=None):
            for k in range(nk):
                if ready is not None and k >= ready[2]:
                    nc.tensor.wait_ge(sem(ready[0]), ready[1] + k + 1)
                last = unit_slice(par_, a_hi, a_lo, k0 + k, k, nk, b)
            return last

        def unit(pe, P, par_, a_hi=h_hi, a_lo=h_lo, nk=KD, ready=None):
            unit_wait(pe, P, par_)
            three_pass(par_, a_hi, a_lo, 0, nk, 2 * par_, ready).then_inc(unit_done, 1)

        def keep_warm(bank, n):
            for _ in range(n):
                nc.tensor.matmul(ps[0:64, bank, 0:128], K("ident")[:, 0:64], K("ones"), start=True, stop=True)

        def barrier(eng, n):
            eng.drain().then_inc(sem("phase%d_over" % n), 1)
            eng.wait_ge(sem("phase%d_over" % n), 3)

        def rsqrt_act(own, src, rx, ry, scale, eps):
            own(nc.scalar.activation(two(rx), src, ACT.Identity, bias=P1("eps", eps), scale=scale))
            own(nc.scalar.activation(ry, rx, ACT.Ln))
            nc.scalar.activation(ry, ry, ACT.Exp, scale=-0.5).then_inc(sem("rsqrt_guess"), 1)
            own.eng.drain()

        def rsqrt_dve(own, dve, n, rx, ry, rt):
            dve.wait_ge(sem("rsqrt_guess"), n)
            own(nc.vector.tensor_tensor(rt, ry, ry, ALU.mult))
            own(nc.vector.scalar_tensor_tensor(rt, rt, -0.5, rx, ALU.mult, ALU.mult))
            own(nc.vector.scalar_tensor_tensor(ry, rt, 1.5, ry, ALU.add, ALU.mult))

        RS_CT, RS_FIN, RS_ATT = 2, 2 + CT, 2 + 2 * CT
        RS_NORM = (0, 1, 2 + 2 * CT + 24)

        SQ = (sq_ffn, sq_ffn, (sA, sR))

        def square(act, m, k, q):
            if not (isinstance(k, int) and k < 2):
                act.wait_ge(sem("sq_summed"), 8 * m + k - 1)
            nc.scalar.activation(SQ[m][q][:, :], x[:, k, :], ACT.Square).then_inc(sem("sq_ready"), 1)
            act.drain()

        def sum_squares(pe, m, k, q, start=False, stop=False):
            pe.wait_ge(sem("sq_ready"), 8 * m + k + 1)
            for c in range(2):
                last = nc.tensor.matmul(ps[:, 4 + c, 0:HC], K("ones"), SQ[m][q][:, c * HC:(c + 1) * HC], start=start, stop=stop)
            last.then_inc(sem("sq_summed"), 1)

        def units_and_squares(pe, m, P0, one):
            one(P0, 0)
            one(P0, 1)
            sum_squares(pe, m, 0, 0, start=True)
            with pe.Fori(1, 4) as j:
                one(P0 + j, 0)
                sum_squares(pe, m, 2 * j - 1, 1)
                one(P0 + j, 1)
                sum_squares(pe, m, 2 * j, 0)
            sum_squares(pe, m, KD - 1, 1, stop=True)

        def splits_and_squares(act, m, P0, words):
            def some(j, w):
                for q in range(2):
                    split_hi(act, P0 + j + 1, q, w)
                    act.wait_ge(evac[q], P0 + j + 1)
                    square(act, m, 2 * j + q, q)

            some(0, words)
            with act.Fori(1, 3) as j:
                some(j, words)
            some(3, W8)

        def first_squares_pe(pe):
            pe.wait_ge(sem("con_loaded"), 32)
            for k in range(KD):
                sum_squares(pe, 0, k, k % 2, start=(k == 0), stop=(k == KD - 1))

        def first_squares_act(act):
            for k in range(KD):
                if k % 2 == 0:
                    act.wait_ge(sem("x_loaded%d" % (k // 2)), 16)
                square(act, 0, k, k % 2)

        def norm_act(act, own, m):
            act.wait_ge(sem("sq_summed"), 8 * m + 8)
            if m == 0:
                act.wait_ge(sem("con_loaded"), 32)
            rsqrt_act(own, bank2(4), nrx[:, :], nry[:, :], 1.0 / D, 0)
            for k in range(KD):
                act.wait_ge(sem("hf_ready"), 8 * m + k + 1)
                nc.scalar.activation(h_hi[:, k, :], hf[k % 2][:, :], ACT.Copy).then_inc(sem("h_hi_ready"), 1)
                act.drain()

        def norm_dve(dve, own, m, gain):
            rsqrt_dve(own, dve, RS_NORM[m] + 1, nrx[:, :], nry[:, :], nrt[:, :])

            def low(k):
                dve.wait_ge(sem("h_hi_ready"), 8 * m + k + 1)
                nc.vector.tensor_tensor(h_lo[:, k, :], hf[k % 2][:, :], h_hi[:, k, :].bitcast(F32),
                                        ALU.subtract).then_inc(sem("h_ready"), 1)
                dve.drain()

            for k in range(KD):
                nc.vector.scalar_tensor_tensor(hf[k % 2][:, :], x[:, k, :], P1(gain, k), nry[:, :],
                                               ALU.mult, ALU.mult).then_inc(sem("hf_ready"), 1)
                dve.drain()
                if k:
                    low(k - 1)
            low(KD - 1)

        def ffn_pe(pe, f, P0):
            def up(half, j0):
                with pe.Fori(j0, HALF) as j:
                    P = P0 + 15 * half + j
                    unit(pe, P, 0)
                    unit(pe, P, 1)

            def down(half):
                first = P0 + 15 * half + HALF
                done = HALF * (2 * f + half)

                def one(P, q):
                    if q == 0:
                        pe.wait_ge(sem("g_ready"), done + HALF - 1)
                    unit(pe, P, q, g_hi, g_lo, HALF, ready=("g_ready", done, HALF - 1))

                if (f, half) == (0, 1):
                    units_and_squares(pe, 1, first, one)
                else:
                    with pe.Fori(0, 4) as j:
                        one(first + j, 0)
                        one(first + j, 1)

            unit(pe, P0, 0, ready=("h_ready", 8 * 2 * f, 0))
            unit(pe, P0, 1)
            up(0, 1)
            down(0)
            up(1, 0)
            down(1)

        def ffn_act(act, f, P0):
            def pair(P, j, words):
                act.wait_ge(unit_done, 2 * P + 1)
                nc.scalar.activation(two(sg[:, :]), bank2(0), ACT.Silu).then_inc(evac[0], 1)
                act.drain()
                split_hi(act, P + 1, 0, words)
                split_hi(act, P + 1, 1, words)
                act.wait_ge(evac[1], P + 1)
                nc.scalar.activation(g_hi[:, j, :], gt[:, :], ACT.Copy).then_inc(sem("g_hi_ready"), 1)
                act.drain()

            def up(half):
                with act.Fori(0, HALF - 1) as j:
                    pair(P0 + 15 * half + j, j, W8)
                pair(P0 + 15 * half + HALF - 1, HALF - 1, W11)

            def down(half):
                first = P0 + 15 * half + HALF
                with act.Fori(1, 4) as j:
                    split_hi(act, first + j, 0, W11)
                    split_hi(act, first + j, 1, W11)
                split_hi(act, first + 4, 0, W8)
                split_hi(act, first + 4, 1, W8)

            if f == 0:
                up(0)
                down(0)
                up(1)
                splits_and_squares(act, 1, P0 + 15 + HALF, W11)
            else:
                with act.Fori(0, 2) as half:
                    up(half)
                    down(half)

        def ffn_dve(dve, f, P0):
            with dve.Fori(0, 2) as half:
                with dve.Fori(0, HALF) as j:
                    P, G = P0 + 15 * half + j, HALF * (2 * f + half) + j
                    dve.wait_ge(unit_done, 2 * P + 2)
                    dve.wait_ge(evac[0], P + 1)
                    nc.vector.tensor_tensor(two(gt[:, :]), two(sg[:, :]), bank2(2), ALU.mult).then_inc(evac[1], 1)
                    dve.drain()
                    dve.wait_ge(evac[1], P + 1)
                    dve.wait_ge(sem("g_hi_ready"), G + 1)
                    nc.vector.tensor_tensor(g_lo[:, j, :], gt[:, :], g_hi[:, j, :].bitcast(F32),
                                            ALU.subtract).then_inc(sem("g_ready"), 1)
                    dve.drain()
                with dve.Fori(0, 4) as j:
                    P = P0 + 15 * half + HALF + j
                    for q in range(2):
                        dve.wait_ge(unit_done, 2 * P + q + 1)
                        dve.wait_ge(evac[q], P)
                        nc.vector.scalar_tensor_tensor(two(x[:, 2 * j + q, :]), bank2(2 * q), 0.5, two(x[:, 2 * j + q, :]),
                                                       ALU.mult, ALU.add).then_inc(evac[q], 1)
                        dve.drain()

        def ffn_pool(pool, P0):
            with pool.Fori(0, 2) as half:
                with pool.Fori(0, HALF) as j:
                    for q in range(2):
                        split_lo(pool, P0 + 15 * half + j, q, W8)
                with pool.Fori(0, 4) as j:
                    for q in range(2):
                        split_lo(pool, P0 + 15 * half + HALF + j, q, W11)

        def copy_cache(sp, g, i):
            rows, drop = PIECE[g], DS if g < 2 else 0
            sp.dma_start(t["cache_out%d" % g][:, bass.ds(i * rows, rows), :], t["cache%d" % g][:, bass.ds(i * rows + drop, rows), :])\
                .then_inc(sem("cache_copied"), 16)

        def ffn_sp(sp, P0, w8_0, w11_0):
            def some(half, j0, j1, down):
                def one(j):
                    for q in range(2):
                        if down:
                            load_unit(sp, P0 + 15 * half + HALF + j, q, t["w11"][w11_0 + 8 * half + 2 * j + q], W11)
                        else:
                            load_unit(sp, P0 + 15 * half + j, q, t["w8"][w8_0 + 22 * half + 2 * j + q], W8)
                    if down:
                        copy_cache(sp, 0 if P0 == 0 else 1, 4 * half + j)
                    else:
                        copy_cache(sp, 2, (-1 if P0 == 0 else 21) + 11 * half + j)
                with sp.Fori(j0, j1) as j:
                    one(j)

            if P0 == 0:
                for q in range(2):
                    load_unit(sp, 0, q, t["w8"][q], W8)
                some(0, 1, HALF, False)
                some(0, 0, 4, True)
                some(1, 0, HALF, False)
                some(1, 0, 4, True)
            else:
                with sp.Fori(0, 2) as half:
                    some(half, 0, HALF, False)
                    some(half, 0, 4, True)

        def units_until(P, q):
            return 2 * P + q + 1

        PRODS = ["A", "D"] + ["A", "D", "D"] * 4 + ["A", "D"] + ["D", "D", "D"]
        NPROD = len(PRODS)
        N_A, N_D = PRODS.count("A"), PRODS.count("D")

        def rw_units(i):
            return [(P_CT + 7 * i[0] + (7 * i[1] + n) // 2, (7 * i[1] + n) % 2, n) for n in range(3)]

        def gate_units(i):
            return [(P_CT + 7 * i[0] + (7 * i[1] + n) // 2, (7 * i[1] + n) % 2) for n in range(3, 7)]

        def tile_of(a, T, h):
            return a[64 * h:64 * h + 64, T * 128:(T + 1) * 128]

        def rwkv_pe(pe):
            unit(pe, P_RW, 0, ready=("h_ready", 8, 0))
            unit(pe, P_RW, 1)
            pe.wait_ge(sem("lora_in_ready"), 2)
            with pe.Fori(0, 2) as cc:
                for c2 in range(2):
                    ct = 2 * cc + c2
                    for P, q, n in rw_units((cc, c2)):
                        unit(pe, P, q)
                    filled = 0

                    def fill(slices):
                        nonlocal filled
                        for _ in range(slices):
                            P, q = gate_units((cc, c2))[filled // KD]
                            k = filled % KD
                            if k == 0:
                                unit_wait(pe, P, q)
                            last = unit_slice(q, h_hi, h_lo, k, k, KD, 2 * q)
                            if k == KD - 1:
                                last.then_inc(unit_done, 1)
                            filled += 1

                    pe.wait_ge(sem("lora_w%d" % c2), 16 * (cc + 1))
                    pe.wait_ge(sem("o_evac"), 1 + ct)
                    for r, b in ((0, 4), (1, 6)):
                        for c in range(2):
                            last = nc.tensor.matmul(ps[:, b + c, 0:HC], LO[c2][64 * r:64 * r + 64, :],
                                                    UW[64 * r:64 * r + 64, c * HC:(c + 1) * HC], start=True, stop=True)
                        last.then_inc(sem("lora_done"), 1)
                    fill(FILL["norm"])
                    pe.wait_ge(sem("kk_sq"), ct + 1)
                    pe.wait_ge(sem("gates_ready"), ct + 1)
                    for c in range(2):
                        last = nc.tensor.matmul(ps[:, 6 + c, 0:HC], K("bones"), TT[:, c * HC:(c + 1) * HC], start=True, stop=True)
                    last.then_inc(sem("kk_norm"), 1)
                    for a, arr, need in ((0, KA, 1), (1, BH, 2), (2, KH, 3), (3, UV, 4)):
                        fill(FILL["tokens"][a])
                        pe.wait_ge(sem("fm_ready"), 4 * ct + need)
                        if a == 2:
                            pe.wait_ge(sem("rsqrt_guess"), RS_CT + ct + 1)
                        for T in range(4):
                            last = nc.tensor.transpose(ps[:, 4 + a, T * 128:(T + 1) * 128], arr[:, T * 128:(T + 1) * 128], K("ident"))
                        last.then_inc(sem("tr_done"), 1)
                    fill(FILL["bonus"])
                    pe.wait_ge(sem("rk_ready"), ct + 1)
                    pe.wait_ge(sem("tok_a"), 2 * ct + 2)
                    for c in range(2):
                        last = nc.tensor.matmul(ps[:, 4 + c, 0:HC], K("bones"), TT[:, c * HC:(c + 1) * HC], start=True, stop=True)
                    last.then_inc(sem("bonus_sum"), 1)
                    done_a, done_d = 0, 0
                    counts = []
                    for kind in PRODS:
                        done_a += kind == "A"
                        done_d += kind == "D"
                        counts.append((kind, done_a, done_d))

                    def bank_free(n, h):
                        if n == 0:
                            pe.wait_ge(sem("bonus_evac"), ct + 1)
                        elif n == 1:
                            pe.wait_ge(sem("tok_d"), 2 * ct + 2)
                        else:
                            read(n - 2, h)

                    def read(n, h):
                        kind, a, d = counts[n]
                        if kind == "A":
                            pe.wait_ge(sem("mat_a%d" % h), N_A * ct + a)
                        else:
                            pe.wait_ge(sem("mat_d%d" % h), N_D * ct + d)

                    def product(n, h, lhs, rhs):
                        for T in range(4):
                            last = nc.tensor.matmul(ps[:, 4 + (2 * n + h) % 4, T * 128:(T + 1) * 128], lhs(T), rhs(T),
                                                    start=True, stop=True)
                        last.then_inc(sem("mat_done%d" % h), 1)

                    def cols(a):
                        return lambda T: a[:, T * 128:(T + 1) * 128]

                    for h in range(2):
                        bank_free(0, h)
                        product(0, h, lambda T: tile_of(KA, T, h), lambda T: tile_of(BH, T, h))
                    for h in range(2):
                        bank_free(1, h)
                        product(1, h, lambda T: tile_of(BH, T, h), lambda T: tile_of(KA, T, h))
                    n = 2
                    for lv in range(5):
                        fill(FILL["level"][lv])
                        for h in range(2):
                            bank_free(n, h)
                            if lv == 0:
                                pe.wait_ge(sem("inv_init%d" % h), ct + 1)
                            else:
                                read(n - 1, h)
                                pe.wait_ge(sem("lm_ready%d" % h), 4 * ct + lv)
                            product(n, h, cols(LM[h]), cols(XT[h]))
                        if lv < 4:
                            for h in range(2):
                                read(n, h)
                                bank_free(n + 1, h)
                                product(n + 1, h, cols(ZZ[h]), cols(XX[h]))
                            for h in range(2):
                                bank_free(n + 2, h)
                                product(n + 2, h, cols(XX[h]), cols(ZZ[h]))
                            n += 3
                        else:
                            for h in range(2):
                                read(n, h)
                                bank_free(n + 1, h)
                                product(n + 1, h, cols(XX[h]), cols(ZZ[h]))
                            n += 2
                    for lhs, rhs in ((KH, KA), (BH, RH), (KH, RH)):
                        for h in range(2):
                            bank_free(n, h)
                            product(n, h, lambda T: tile_of(lhs, T, h), lambda T: tile_of(rhs, T, h))
                        n += 1
                    assert n == NPROD
                    for h in range(2):
                        read(NPROD - 3, h)
                        read(NPROD - 2, h)
                        for T in range(4):
                            last = nc.tensor.matmul(ps[:, 6, T * 128 + 64 * h:T * 128 + 64 * h + 64], ZZ[h][:, T * 128:(T + 1) * 128],
                                                    TOK[:, 3, T, 64 * h:64 * h + 64], start=True, stop=True)
                    last.then_inc(sem("mv_done"), 1)
                    for h in range(2):
                        read(NPROD - 1, h)
                        for T in range(4):
                            last = nc.tensor.matmul(ps[64 * h:64 * h + 64, 4, T * 128:(T + 1) * 128], TOK[:, 0, T, 64 * h:64 * h + 64],
                                                    XT[h][:, T * 128:(T + 1) * 128], start=True, stop=True)
                    last.then_inc(sem("xk_done"), 1)
                    fill(FILL["mv"])
                    pe.wait_ge(sem("mv_evac"), ct + 1)
                    for h in range(2):
                        for T in range(4):
                            last = nc.tensor.matmul(ps[:, 7, T * 128 + 64 * h:T * 128 + 64 * h + 64], XT[h][:, T * 128:(T + 1) * 128],
                                                    MV[:, T, 64 * h:64 * h + 64], start=True, stop=True)
                    last.then_inc(sem("w1_done"), 1)
                    fill(FILL["xk"])
                    pe.wait_ge(sem("xk_evac"), ct + 1)
                    pe.wait_ge(sem("w1_evac"), ct + 1)
                    for ch in range(NCH):
                        r0, T = 64 * (ch % 2), ch // 2
                        pe.wait_ge(sem("st_ready"), 1 + NCH * ct + ch)
                        for h in range(2):
                            last = nc.tensor.matmul(ps[:, 4 + h, 0:64], XK[64 * h:64 * h + 64, 128 * T:128 * T + 128],
                                                    ST[64 * h:64 * h + 64, ch, :], start=True, stop=True)
                        last.then_inc(sem("u_done"), 1)
                        nc.tensor.matmul(ps[:, 6, 0:128], TOK[r0:r0 + 64, 2, T, :], TOK[r0:r0 + 64, 3, T, :], start=True, stop=False)
                        fill(FILL["chunk"][ch])
                        pe.wait_ge(sem("u_ready"), NCH * ct + ch + 1)
                        last = nc.tensor.matmul(ps[:, 6, 0:128], TOK[r0:r0 + 64, 1, T, :], UU[r0:r0 + 64, T, :], start=False, stop=True)
                        last.then_inc(sem("ds_done"), 1)
                    assert filled == 4 * KD
                    for h in range(2):
                        rows = slice(64 * h, 64 * h + 64)
                        for T in range(4):
                            o = ps[rows, 7, T * 128:(T + 1) * 128]
                            nc.tensor.matmul(o, UU[:, T, rows], LR[h][:, T * 128:(T + 1) * 128], start=(T == 0), stop=False,
                                             skip_group_check=True)
                            nc.tensor.matmul(o, TOK[:, 3, T, rows], LM[h][:, T * 128:(T + 1) * 128], start=False, stop=False,
                                             skip_group_check=True)
                            for e in range(2):
                                ch = 2 * T + e
                                last = nc.tensor.matmul(ps[rows, 7, ch * 64:ch * 64 + 64], ST[rows, ch, :], RH[rows, ch * 64:ch * 64 + 64],
                                                        start=False, stop=True, skip_group_check=True)
                    last.then_inc(sem("o_done"), 1)

        def rwkv_act(act, own):
            def take(P, q, n, e, tile):
                act.wait_ge(unit_done, units_until(P, q))
                if not (isinstance(e, int) and e < 2):
                    act.wait_ge(sem("mixed"), e - 1)
                nc.scalar.activation(two(PR[q][:, :]), bank2(2 * q), ACT.Copy).then_inc(evac[q], 1)
                act.drain()
                act.wait_ge(evac[q], P + 1)
                nc.scalar.activation(SH[:, tile, :], PR[q][:, SEQ - 1:NT:DS], ACT.Copy).then_inc(sem("shift_kept"), 1)
                act.drain()
                split_hi(act, P + 1, q, W8)

            take(P_RW, 0, 0, 0, 12)
            take(P_RW, 1, 1, 1, 13)
            act.wait_ge(sem("mixed"), 1)
            nc.scalar.activation(UW[0:64, :], UW[0:64, :], ACT.Tanh).then_inc(sem("lora_in_ready"), 1)
            act.drain()
            act.wait_ge(sem("mixed"), 2)
            nc.scalar.activation(UG[:, :], UG[:, :], ACT.Sigmoid).then_inc(sem("lora_in_ready"), 1)
            act.drain()
            with act.Fori(0, 2) as cc:
                own.enter(cc, 2 * 5)
                for c2 in range(2):
                    ct = 2 * cc + c2
                    for P, q, n in rw_units((cc, c2)):
                        take(P, q, n, 2 + 6 * cc + 3 * c2 + n, 4 * n + ct)

                    def gate_out(n):
                        P, q = gate_units((cc, c2))[n]
                        act.wait_ge(unit_done, units_until(P, q))
                        if n >= 2:
                            act.wait_ge(sem("gate_stored%d" % q), 16 * (2 * ct + 1))
                        nc.scalar.activation(two(GS[q][:, :]), bank2(2 * q), ACT.Copy).then_inc(evac[q], 1)
                        split_hi(act, P + 1, q, W8)
                        act.wait_ge(evac[q], P + 1)
                        act.dma_start(t["gates"][4 * ct + n], GS[q][:, :]).then_inc(sem("gate_stored%d" % q), 16)

                    act.wait_ge(sem("lora_done"), 1 + 2 * ct + 1)
                    nc.scalar.activation(two(SW[:, :]), bank2(4), ACT.Sigmoid, bias=P1("w0", ct))
                    act.wait_ge(sem("lora_done"), 1 + 2 * ct + 2)
                    nc.scalar.activation(two(AA[:, :]), bank2(6), ACT.Sigmoid, bias=P1("a0", ct)).then_inc(sem("gates_ready"), 1)
                    act.drain()
                    act.wait_ge(sem("kkr_ready"), ct + 1)
                    nc.scalar.activation(TT[:, :], KA, ACT.Square).then_inc(sem("kk_sq"), 1)
                    act.drain()
                    act.wait_ge(sem("cum_ready"), ct + 1)
                    own(nc.scalar.activation(EP[:, :], CC[:, :], ACT.Exp, scale=-C0))
                    own(nc.scalar.activation(EM[:, :], CC[:, :], ACT.Exp, scale=C0))
                    nc.scalar.activation(CX[:, :], CX[:, :], ACT.Exp, scale=-C0).then_inc(sem("exps_ready"), 1)
                    act.drain()
                    act.wait_ge(sem("kk_norm"), ct + 1)
                    rsqrt_act(own, bank2(6), CC[:, :], SW[:, :], 1.0, 1)
                    gate_out(0)
                    for a in range(2):
                        act.wait_ge(sem("tr_done"), 4 * ct + a + 1)
                        nc.scalar.activation(TOK[:, a].rearrange("p t n -> p (t n)"), ps[:, 4 + a, :], ACT.Copy).then_inc(sem("tok_a"), 1)
                        act.drain()
                    gate_out(1)
                    act.wait_ge(sem("fm_ready"), 4 * ct + 4)
                    nc.scalar.activation(SV[:, ct], FM[:, :, SEQ:NT], ACT.Copy)
                    own(nc.scalar.activation(SVP[:, ct], EP[:, SEQ + DS - 1:NT:DS], ACT.Copy))
                    for h in range(2):
                        act.wait_ge(sem("mat_done%d" % h), NPROD * ct + 1)
                        nc.scalar.activation(LR[h][:, :], ps[:, 4 + h, :], ACT.Copy).then_inc(sem("mat_a%d" % h), 1)
                        act.drain()
                    for lv in range(5):
                        n = 2 + 3 * lv
                        for h in range(2):
                            act.wait_ge(sem("mat_done%d" % h), NPROD * ct + n + 1)
                            nc.scalar.activation(ZZ[h][:, :], ps[:, 4 + (2 * n + h) % 4, :], ACT.Copy).then_inc(sem("mat_a%d" % h), 1)
                            act.drain()
                    act.wait_ge(sem("mv_done"), ct + 1)
                    nc.scalar.activation(MV[:, :, :].rearrange("p t n -> p (t n)"), ps[:, 6, :], ACT.Copy).then_inc(sem("mv_evac"), 1)
                    act.drain()
                    act.wait_ge(sem("w1_done"), ct + 1)
                    nc.scalar.activation(W1[:, :, :].rearrange("p t n -> p (t n)"), ps[:, 7, :], ACT.Copy).then_inc(sem("w1_evac"), 1)
                    act.drain()
                    gate_out(2)
                    act.wait_ge(sem("st_ready"), 1 + NCH * ct + NCH)
                    act.dma_start(t["wkv_p"][ct], ST[:, NCH, :]).then_inc(sem("wkvp_stored"), 16)
                    act.wait_ge(sem("o_done"), ct + 1)
                    nc.scalar.activation(o_rw[:, ct, 0:SEQ], ps[:, 7, :], ACT.Copy).then_inc(sem("o_evac"), 1)
                    act.drain()
                    gate_out(3)
                    for q in range(2):
                        act.wait_ge(sem("gate_stored%d" % q), 16 * (2 * ct + 2))
                    act.wait_ge(sem("wkvp_stored"), 16 * (ct + 1))
                own.leave(2)
            act.wait_ge(sem("shift_kept"), SHT)
            act.dma_start(t["shift"], SH[:, :, :]).then_inc(sem("shift_stored"), 16)

        def rwkv_dve(dve, own):
            V = nc.vector
            dve.wait_ge(sem("masks_loaded"), 16)
            V.memset(ST[:, 0, :], 0.0).then_inc(sem("st_ready"), 1)
            dve.drain()
            dve.wait_ge(sem("rw_loaded"), 32)

            def mix(P, q, out, mu, tile):
                p = PR[q]
                dve.wait_ge(evac[q], P + 1)
                V.tensor_tensor(out[:, 1:SEQ], p[:, 0:SEQ - 1], p[:, 1:SEQ], ALU.subtract)
                V.tensor_scalar(out[:, 0:1], p[:, 0:1], -1.0, None, ALU.mult)
                s, so = (a[:, SEQ:NT].rearrange("p (b t) -> p b t", t=DS) for a in (p, out))
                V.tensor_tensor(so[:, :, 1:DS], s[:, :, 0:DS - 1], s[:, :, 1:DS], ALU.subtract)
                own(V.tensor_tensor(so[:, :, 0], SH0[:, tile, :], s[:, :, 0], ALU.subtract))
                V.scalar_tensor_tensor(out, out, mu, p[:, :], ALU.mult, ALU.add).then_inc(sem("mixed"), 1)
                dve.drain()

            mix(P_RW, 0, UW[:, :], P1("mu", 12), 12)
            mix(P_RW, 1, UG[:, :], P1("mu", 13), 13)
            with dve.Fori(0, 2) as cc:
                own.enter(cc, RW_OWN)
                for c2 in range(2):
                    ct = 2 * cc + c2
                    for (P, q, n), out in zip(rw_units((cc, c2)), (UR[:, :], UK[:, :], UV)):
                        mix(P, q, out, P1("mu", 4 * n + ct), 4 * n + ct)
                    dve.wait_ge(sem("mixed"), 2 + 3 * (ct + 1))
                    V.tensor_scalar(KA, UK[:, :], P1("kk", ct), None, ALU.mult).then_inc(sem("kkr_ready"), 1)
                    dve.drain()
                    dve.wait_ge(sem("gates_ready"), ct + 1)
                    own(V.tensor_tensor_scan(CC[:, :], K("reset"), SW[:, :], 0.0, ALU.mult, ALU.add))
                    V.tensor_tensor(CX[:, :], CC[:, :], SW[:, :], ALU.subtract).then_inc(sem("cum_ready"), 1)
                    dve.drain()
                    own(V.tensor_scalar(BH, AA[:, :], 1.0, P1("ka", ct), ALU.subtract, ALU.mult))
                    own(V.scalar_tensor_tensor(UK[:, :], BH, 1.0, UK[:, :], ALU.add, ALU.mult))
                    rsqrt_dve(own, dve, RS_CT + ct + 1, CC[:, :], SW[:, :], TT[:, :])
                    own(V.tensor_tensor(TT[:, :], KA, SW[:, :], ALU.mult))
                    dve.wait_ge(sem("exps_ready"), ct + 1)
                    V.tensor_tensor(KA, TT[:, :], CX[:, :], ALU.mult).then_inc(sem("fm_ready"), 1)
                    dve.drain()
                    own(V.tensor_tensor(TT[:, :], TT[:, :], AA[:, :], ALU.mult))
                    V.scalar_tensor_tensor(BH, TT[:, :], -1.0, EM[:, :], ALU.mult, ALU.mult).then_inc(sem("fm_ready"), 1)
                    dve.drain()
                    V.tensor_tensor(KH, UK[:, :], EM[:, :], ALU.mult).then_inc(sem("fm_ready"), 1)
                    dve.drain()
                    V.tensor_tensor(RH, UR[:, :], EP[:, :], ALU.mult).then_inc(sem("fm_ready"), 1)
                    dve.drain()
                    V.scalar_tensor_tensor(TT[:, :], UR[:, :], P1("rk", ct), UK[:, :], ALU.mult, ALU.mult).then_inc(sem("rk_ready"), 1)
                    dve.drain()
                    for a in range(2, 4):
                        dve.wait_ge(sem("tr_done"), 4 * ct + a + 1)
                        V.tensor_copy(TOK[:, a].rearrange("p t n -> p (t n)"), ps[:, 4 + a, :]).then_inc(sem("tok_d"), 1)
                        dve.drain()
                    dve.wait_ge(sem("bonus_sum"), ct + 1)
                    V.tensor_tensor(two(BN[:, ct]), bank2(4), two(UV), ALU.mult).then_inc(sem("bonus_evac"), 1)
                    dve.drain()

                    def by_tile(a):
                        return a.rearrange("p (t n) -> p t n", t=4)

                    def mask(name):
                        return K(name).unsqueeze(1).to_broadcast([128, 4, 128])

                    n_d = [0, 0]

                    def evac_d(h, ins):
                        ins.then_inc(sem("mat_d%d" % h), 1)
                        dve.drain()
                        n_d[h] += 1

                    def my(h):
                        dve.wait_ge(sem("mat_d%d" % h), N_D * ct + n_d[h])

                    for h in range(2):
                        dve.wait_ge(sem("mat_done%d" % h), NPROD * ct + 2)
                        evac_d(h, V.tensor_tensor(by_tile(XT[h][:, :]), by_tile(ps[:, 6 + h, :]), mask("m2T"), ALU.mult))
                        dve.wait_ge(sem("mat_a%d" % h), N_A * ct + 1)
                        own(V.tensor_tensor(by_tile(XX[h][:, :]), by_tile(LR[h][:, :]), mask("m2"), ALU.mult))
                        V.tensor_tensor(by_tile(XX[h][:, :]), by_tile(XX[h][:, :]), mask("ident"), ALU.add)
                        my(h)
                        V.tensor_tensor(by_tile(XT[h][:, :]), by_tile(XT[h][:, :]), mask("ident"), ALU.add)
                        V.tensor_tensor(by_tile(LM[h][:, :]), by_tile(LR[h][:, :]), mask(LEVELS[0]), ALU.mult)\
                            .then_inc(sem("inv_init%d" % h), 1)
                        dve.drain()
                    for lv in range(5):
                        n = 2 + 3 * lv
                        if lv < 4:
                            for h in range(2):
                                dve.wait_ge(sem("mat_done%d" % h), NPROD * ct + n + 1)
                                V.tensor_tensor(by_tile(LM[h][:, :]), by_tile(LR[h][:, :]), mask(LEVELS[lv + 1]), ALU.mult)\
                                    .then_inc(sem("lm_ready%d" % h), 1)
                                dve.drain()
                            for h in range(2):
                                dve.wait_ge(sem("mat_done%d" % h), NPROD * ct + n + 3)
                                if lv == 0:
                                    dve.wait_ge(sem("inv_init%d" % h), ct + 1)
                                else:
                                    my(h)
                                evac_d(h, V.tensor_tensor(XX[h][:, :], XX[h][:, :], ps[:, 4 + (2 * n + 2 + h) % 4, :], ALU.add))
                                evac_d(h, V.tensor_tensor(XT[h][:, :], XT[h][:, :], ps[:, 4 + (2 * n + 4 + h) % 4, :], ALU.add))
                        else:
                            for h in range(2):
                                dve.wait_ge(sem("mat_done%d" % h), NPROD * ct + n + 2)
                                my(h)
                                evac_d(h, V.tensor_tensor(XT[h][:, :], XT[h][:, :], ps[:, 4 + (2 * n + 2 + h) % 4, :], ALU.add))
                    for n, out, m in ((NPROD - 3, ZZ, "SU"), (NPROD - 2, LR, "IU"), (NPROD - 1, LM, "IU")):
                        for h in range(2):
                            dve.wait_ge(sem("mat_done%d" % h), NPROD * ct + n + 1)
                            evac_d(h, V.tensor_tensor(by_tile(out[h][:, :]), by_tile(ps[:, 4 + (2 * n + h) % 4, :]), mask(m), ALU.mult))
                    assert n_d == [N_D, N_D]
                    dve.wait_ge(sem("xk_done"), ct + 1)
                    V.tensor_copy(XK[:, :], ps[:, 4, :]).then_inc(sem("xk_evac"), 1)
                    dve.drain()
                    dve.wait_ge(sem("w1_evac"), ct + 1)
                    for ch in range(NCH):
                        r0, T = 64 * (ch % 2), ch // 2
                        end = EP[:, 64 * ch + 63:64 * ch + 64]
                        dve.wait_ge(sem("st_ready"), 1 + NCH * ct + ch)
                        own(V.tensor_scalar(STP[:, :], ST[:, ch, :], end, None, ALU.mult))
                        dve.wait_ge(sem("u_done"), NCH * ct + ch + 1)
                        V.tensor_tensor(UU[r0:r0 + 64, T, :].rearrange("p (h n) -> p h n", h=2), ps[r0:r0 + 64, 4:6, 0:64],
                                        W1[r0:r0 + 64, T, :].rearrange("p (h n) -> p h n", h=2), ALU.add)\
                            .then_inc(sem("u_ready"), 1)
                        dve.drain()
                        dve.wait_ge(sem("ds_done"), NCH * ct + ch + 1)
                        for h in range(2):
                            r = slice(64 * h, 64 * h + 64)
                            ins = V.scalar_tensor_tensor(ST[r, ch + 1, :], ps[r, 6, r], end[r], STP[r, :], ALU.mult, ALU.add)
                        ins.then_inc(sem("st_ready"), 1)
                        dve.drain()
                own.leave(2)

        RW_OWN = 2 * (3 + 1 + 2 + 3 + 1 + 1 + 2 + NCH)

        HEADS = [(ct, h) for ct in range(CT) for h in range(2)]

        def hc(ct, h):
            return slice(128 * ct + 64 * h, 128 * ct + 64 * h + 64)

        def mc(ct, h):
            return slice(256 * h + 64 * ct, 256 * h + 64 * ct + 64)

        def rows_of(h):
            return slice(64 * h, 64 * h + 64)

        def rwsam_pe(pe):
            def heads(bank, lhs, rhs, where=mc):
                for ct, h in HEADS:
                    last = nc.tensor.matmul(ps[0:64, bank, where(ct, h)], lhs(ct, h), rhs(ct, h), start=True, stop=True)
                last.then_inc(sem("smat"), 1)

            def scores(bank, a, b):
                for ct, h in HEADS:
                    last = nc.tensor.matmul(ps[0:64, bank + h, 64 * ct:64 * ct + 64], SV[rows_of(h), ct, a, :], SV[rows_of(h), ct, b, :],
                                            start=True, stop=True)
                last.then_inc(sem("smat"), 1)

            def mm(a):
                return lambda ct, h: a[:, mc(ct, h)]

            def tm(a):
                return lambda ct, h: a[:, hc(ct, h)]

            for i, a in enumerate((0, 1, 2, 4)):
                for ct in range(CT):
                    last = nc.tensor.transpose(ps[0:64, 4 + i, 128 * ct:128 * ct + 128], SV[:, ct, a, :], K("ident"))
                last.then_inc(sem("s_tr"), 1)
            scores(0, 0, 1)
            scores(2, 1, 0)
            pe.wait_ge(sem("s_inv"), 1)
            pe.wait_ge(sem("s_tok_d"), 2)
            heads(6, mm(SLM), mm(SXT))
            pe.wait_ge(sem("s_act"), 2)
            heads(7, mm(SZZ), mm(SXX))
            heads(4, mm(SXX), mm(SZZ))
            pe.wait_ge(sem("s_inv"), 2)
            heads(6, mm(SLM), mm(SXT))
            pe.wait_ge(sem("s_act"), 3)
            heads(7, mm(SXX), mm(SZZ))
            scores(0, 2, 0)
            scores(2, 1, 3)
            scores(4, 2, 3)
            pe.wait_ge(sem("s_dve"), 1)
            pe.wait_ge(sem("s_dve"), 2)
            heads(7, mm(SMK), tm(TOS[3]), hc)
            pe.wait_ge(sem("s_dve"), 4)
            for ct, h in HEADS:
                last = nc.tensor.matmul(ps[rows_of(h), 5, 64 * ct:64 * ct + 64], TOS[0][:, hc(ct, h)], SXT[:, mc(ct, h)],
                                        start=True, stop=True)
            last.then_inc(sem("smat"), 1)
            pe.wait_ge(sem("s_act"), 4)
            heads(4, mm(SXT), tm(SMV), hc)
            pe.wait_ge(sem("s_dve"), 5)
            pe.wait_ge(sem("s_states"), 16)
            for ct, h in HEADS:
                for b in range(DB):
                    c = slice(64 * ct + 8 * b, 64 * ct + 8 * b + 8)
                    last = nc.tensor.matmul(ps[rows_of(h), 6, c], SST[rows_of(h), ct, 64 * b:64 * b + 64], SXK[rows_of(h), c],
                                            start=True, stop=True)
            last.then_inc(sem("smat"), 1)
            pe.wait_ge(sem("s_act"), 6)
            for ct in range(CT):
                last = nc.tensor.transpose(ps[0:64, 7, 128 * ct:128 * ct + 128], SU0[:, 64 * ct:64 * ct + 64], K("ident"))
            last.then_inc(sem("smat"), 1)
            pe.wait_ge(sem("s_dve"), 6)
            for h in range(2):
                for ct in range(CT):
                    o = ps[rows_of(h), 4, 64 * ct:64 * ct + 64]
                    nc.tensor.matmul(o, SUU[:, hc(ct, h)], SNB[:, mc(ct, h)], start=(ct == 0), stop=False, skip_group_check=True)
                    nc.tensor.matmul(o, TOS[3][:, hc(ct, h)], SNK[:, mc(ct, h)], start=False, stop=True, skip_group_check=True)
                    for b in range(DB):
                        c = slice(64 * ct + 8 * b, 64 * ct + 8 * b + 8)
                        last = nc.tensor.matmul(ps[rows_of(h), 0, c], SST[rows_of(h), ct, 64 * b:64 * b + 64],
                                                SV[rows_of(h), ct, 3, 8 * b:8 * b + 8], start=True, stop=True)
            last.then_inc(sem("smat"), 1)
            for ct, h in HEADS:
                pe.wait_ge(sem("s_spread"), 2 * ct + h + 1)
                if ct >= 2:
                    pe.wait_ge(sem("s_new"), ct - 1)
                o = ps[rows_of(h), 5 + ct % 2, :]
                nc.tensor.matmul(o, TOS[1][:, hc(ct, h)], SPREAD[h][0], start=True, stop=False)
                nc.tensor.matmul(o, TOS[2][:, hc(ct, h)], SPREAD[h][1], start=False, stop=True).then_inc(sem("s_dstate"), 1)

        def rwsam_act(act, own):
            def take(need, out, src):
                act.wait_ge(sem("smat"), need)
                nc.scalar.activation(out, src, ACT.Copy).then_inc(sem("s_act"), 1)
                act.drain()

            for i in range(2):
                act.wait_ge(sem("s_tr"), i + 1)
                nc.scalar.activation(TOS[i], ps[0:64, 4 + i, :], ACT.Copy).then_inc(sem("s_tok_a"), 1)
                act.drain()
            take(1, SLR.rearrange("p (h n) -> p h n", h=2), ps[0:64, 0:2, 0:256])
            take(3, SZZ, ps[0:64, 6, :])
            take(6, SZZ, ps[0:64, 6, :])
            take(11, SMV, ps[0:64, 7, :])
            take(13, SW1, ps[0:64, 4, :])
            take(14, SU0, ps[:, 6, 0:256])
            act.wait_ge(sem("smat"), 16)
            nc.scalar.activation(o_rw[:, :, SEQ:NT], ps[:, 4, 0:256].rearrange("p (c n) -> p c n", c=CT), ACT.Copy)\
                .then_inc(sem("o_new"), 1)
            act.drain()
            for ct in range(CT):
                act.wait_ge(sem("s_new"), ct + 1)
                act.dma_start(t["wkv_s"][ct], SST[:, ct, :]).then_inc(sem("wkvs_stored"), 16)

        def rwsam_dve(dve, own):
            V = nc.vector

            def by_head(a):
                return a.rearrange("p (h n) -> p h n", h=8)

            def mask(name):
                return K(name, 64)[:, 0:64].unsqueeze(1).to_broadcast([64, 8, 64])

            def by_pair(a):
                return a.rearrange("p (h c n) -> p h c n", h=2, c=CT)

            def score_banks(b):
                return ps[0:64, b:b + 2, 0:256].rearrange("p h (c n) -> p h c n", c=CT)

            def mask4(name):
                return K(name, 64)[:, 0:64].unsqueeze(1).unsqueeze(1).to_broadcast([64, 2, CT, 64])

            for i in range(2, 4):
                dve.wait_ge(sem("s_tr"), i + 1)
                V.tensor_copy(TOS[i], ps[0:64, 4 + i, :]).then_inc(sem("s_tok_d"), 1)
                dve.drain()
            dve.wait_ge(sem("smat"), 2)
            own(V.tensor_tensor(by_pair(SXT), score_banks(2), mask4("m2T"), ALU.mult))
            dve.wait_ge(sem("s_act"), 1)
            own(V.tensor_tensor(by_head(SXX), by_head(SLR), mask("m2"), ALU.mult))
            V.tensor_tensor(by_head(SXX), by_head(SXX), mask("ident"), ALU.add)
            V.tensor_tensor(by_head(SXT), by_head(SXT), mask("ident"), ALU.add)
            V.tensor_tensor(by_head(SLM), by_head(SLR), mask("m4"), ALU.mult).then_inc(sem("s_inv"), 1)
            dve.drain()
            dve.wait_ge(sem("s_inv"), 1)
            dve.wait_ge(sem("smat"), 5)
            V.tensor_tensor(SXX, SXX, ps[0:64, 7, :], ALU.add)
            V.tensor_tensor(SXT, SXT, ps[0:64, 4, :], ALU.add)
            V.tensor_tensor(by_head(SLM), by_head(SLR), mask("m8"), ALU.mult).then_inc(sem("s_inv"), 1)
            dve.drain()
            dve.wait_ge(sem("s_inv"), 2)
            dve.wait_ge(sem("smat"), 7)
            V.tensor_tensor(SXT, SXT, ps[0:64, 7, :], ALU.add).then_inc(sem("s_dve"), 1)
            dve.drain()
            for i, (out, m) in enumerate(((SMK, "SU8"), (SNB, "IU8"), (SNK, "IU8"))):
                dve.wait_ge(sem("smat"), 8 + i)
                V.tensor_tensor(by_pair(out), score_banks(2 * i), mask4(m), ALU.mult).then_inc(sem("s_dve"), 1)
                dve.drain()
            dve.wait_ge(sem("smat"), 12)
            V.tensor_copy(SXK, ps[:, 5, 0:256]).then_inc(sem("s_dve"), 1)
            dve.drain()
            dve.wait_ge(sem("smat"), 15)
            dve.wait_ge(sem("s_act"), 5)
            V.tensor_tensor(SUU, SW1, ps[0:64, 7, :], ALU.add).then_inc(sem("s_dve"), 1)
            dve.drain()
            dve.wait_ge(sem("s_dve"), 6)
            dve.wait_ge(sem("smat"), 16)
            dve.wait_ge(sem("s_tok_d"), 2)
            dve.wait_ge(sem("o_new"), 1)
            V.tensor_tensor(o_rw[:, :, SEQ:NT], o_rw[:, :, SEQ:NT], ps[:, 0, 0:256].rearrange("p (c n) -> p c n", c=CT), ALU.add)\
                .then_inc(sem("o_sample"), 1)
            dve.drain()
            seq = K("seq", 64).unsqueeze(2).to_broadcast([64, 8, 64])
            for ct in range(CT):
                for h in range(2):
                    if ct:
                        dve.wait_ge(sem("s_dstate"), 2 * ct + h - 1)
                    for a, src in ((0, SUU), (1, TOS[3])):
                        ins = V.tensor_tensor(by_head(SPREAD[h][a]), src[:, hc(ct, h)].unsqueeze(1).to_broadcast([64, 8, 64]),
                                              seq, ALU.mult)
                    ins.then_inc(sem("s_spread"), 1)
                    dve.drain()
                if ct:
                    new_state(dve, own, ct - 1)
            new_state(dve, own, CT - 1)

        def new_state(dve, own, ct):
            V = nc.vector
            dve.wait_ge(sem("s_dstate"), 2 * ct + 2)
            own(V.tensor_tensor(SST[:, ct, :], SST[:, ct, :], ps[:, 5 + ct % 2, :], ALU.add))
            s3 = SST[:, ct, :].rearrange("p (b n) -> p b n", b=DB)
            V.tensor_tensor(s3, s3, SVP[:, ct, :].unsqueeze(2).to_broadcast([128, DB, DH]), ALU.mult).then_inc(sem("s_new"), 1)
            dve.drain()

        FO, FS, FX, FY, FT = (EP, UR), (EM, UK), (CC, SW), (CX, AA), TT

        def rwout_pe(pe):
            def mean(ct):
                if ct == 0:
                    pe.wait_ge(sem("o_sample"), 1)
                    pe.wait_ge(sem("s_new"), CT)
                else:
                    pe.wait_ge(sem("ln_centred"), ct)
                for c in range(2):
                    last = nc.tensor.matmul(ps[:, 4 + c, 0:HC], K("bones"), o_rw[:, ct, c * HC:(c + 1) * HC], start=True, stop=True)
                last.then_inc(sem("ln_mean"), 1)

            def var(ct):
                pe.wait_ge(sem("ln_sq"), ct + 1)
                if ct:
                    pe.wait_ge(sem("rsqrt_guess"), RS_FIN + ct)
                for c in range(2):
                    last = nc.tensor.matmul(ps[:, 6 + c, 0:HC], K("bones"), FS[ct % 2][:, c * HC:(c + 1) * HC], start=True, stop=True)
                last.then_inc(sem("ln_var"), 1)

            def gate(ct):
                if ct >= 2:
                    pe.wait_ge(sem("rw_out"), ct - 1)
                for c in range(2):
                    last = nc.tensor.matmul(ps[:, 2 * (ct % 2) + c, 0:HC], GL[:, 128 * ct:128 * ct + 128], UG[:, c * HC:(c + 1) * HC],
                                            start=True, stop=True)
                last.then_inc(sem("gate_lora"), 1)

            mean(0)
            gate(0)
            for ct in range(CT):
                if ct + 1 < CT:
                    mean(ct + 1)
                var(ct)
                if ct + 1 < CT:
                    gate(ct + 1)

        def rwout_act(act, own):
            def square(ct):
                act.wait_ge(sem("ln_centred"), ct + 1)
                if ct >= 2:
                    act.wait_ge(sem("ln_var"), ct - 1)
                nc.scalar.activation(FS[ct % 2][:, :], FO[ct % 2][:, :], ACT.Square).then_inc(sem("ln_sq"), 1)
                act.drain()

            square(0)
            for ct in range(CT):
                if ct + 1 < CT:
                    square(ct + 1)
                act.wait_ge(sem("ln_var"), ct + 1)
                if ct >= 2:
                    act.wait_ge(sem("rw_out"), ct - 1)
                rsqrt_act(own, bank2(6), FX[ct % 2][:, :], FY[ct % 2][:, :], 1.0 / DH, 2)

        def rwout_dve(dve, own):
            V = nc.vector

            def centre(ct):
                dve.wait_ge(sem("ln_mean"), ct + 1)
                if ct >= 2:
                    dve.wait_ge(sem("ln_sq"), ct - 1)
                V.scalar_tensor_tensor(two(FO[ct % 2][:, :]), bank2(4), -1.0 / DH, two(o_rw[:, ct, :]), ALU.mult, ALU.add)\
                    .then_inc(sem("ln_centred"), 1)
                dve.drain()

            centre(0)
            for ct in range(CT):
                if ct + 1 < CT:
                    centre(ct + 1)
                rsqrt_dve(own, dve, RS_FIN + ct + 1, FX[ct % 2][:, :], FY[ct % 2][:, :], FT[:, :])
                own(V.tensor_tensor(FT[:, :], FO[ct % 2][:, :], FY[ct % 2][:, :], ALU.mult))
                own(V.tensor_scalar(FT[:, :], FT[:, :], P1("lng", ct), P1("lnb", ct), ALU.mult, ALU.add))
                own(V.tensor_tensor(FT[:, :], FT[:, :], BN[:, ct, :], ALU.add))
                dve.wait_ge(sem("gate_lora"), ct + 1)
                V.tensor_tensor(two(o_rw[:, ct, :]), two(FT[:, :]), bank2(2 * (ct % 2)), ALU.mult).then_inc(sem("rw_out"), 1)
                dve.drain()

        def at_units(cc, c2):
            return [(P_ATT + 9 * cc + (9 * c2 + n) // 2, (9 * c2 + n) % 2, n) for n in range(9)]

        ITS = [(h, n) for h in range(2) for n in range(4)]

        def widths(n):
            return (128 if n == 0 else 256, 128 * (n + 1), 128 * (n + 1))

        def key_tiles(n):
            return ([(0, k) for k in range(max(0, n - 1), n + 1)] + [(g, k) for g in (1, 2) for k in range(n + 1)])

        def batches(tiles):
            return [tiles[i:i + 4] for i in range(0, len(tiles), 4)]

        NBAT = [len(batches(key_tiles(n))) for _, n in ITS]
        PER = sum(NBAT) + 3
        SBANK = ((4, 5, 6), (1, 2, 3))
        TBANK = (0, 7)
        STILES = ([(0, 128)] + [(KOFF[1] + 128 * i, 128) for i in range(4)] + [(KOFF[2] + 128 * i, 128) for i in range(4)]
                  + [(128 + 64 * g, 64) for g in range(3)])

        def q_index(n):
            return sum(kind < 2 for _, kind in QKV_ORDER[:n])

        def att_pe(pe):
            with pe.Fori(0, 2) as cc:
                for c2 in range(2):
                    hp = 2 * cc + c2
                    us = at_units(cc, c2)

                    def post(n):
                        g, kind = QKV_ORDER[n]
                        if kind < 2:
                            i = q_index(n)
                            pe.wait_ge(sem("qk_sq"), 6 * hp + i + 1)
                            pe.wait_ge(sem("rsqrt_guess"), RS_ATT + 6 * hp + i)
                            if n == 0:
                                pe.wait_ge(sem("so_evac"), 1 + hp)
                            for c in range(2):
                                last = nc.tensor.matmul(ps[:, 4 + c, 0:HC], K("bones"), asq[:, c * HC:(c + 1) * HC],
                                                        start=True, stop=True)
                            last.then_inc(sem("qk_norm"), 1)
                        else:
                            pe.wait_ge(evac[us[n][1]], us[n][0] + 1)
                            pe.wait_ge(sem("v_evac"), 1 + 3 * hp + g)
                            for T in range(4):
                                nc.tensor.transpose(ps[:, 6, 128 * T:128 * T + 128], QKV[:, g, 2, 128 * T:128 * T + 128], K("ident"))
                            nc.tensor.transpose(ps[0:64, 7, 0:128], QKV[:, g, 2, SEQ:NT], K("ident")).then_inc(sem("v_tr"), 1)

                    for P, q, n in us:
                        unit(pe, P, q)
                        if n:
                            post(n - 1)
                    post(8)
                    pe.wait_ge(sem("qk_applied"), 1 + 6 * hp + 6)
                    pe.wait_ge(sem("v_evac"), 1 + 3 * hp + 3)
                    for q in range(2):
                        last_u = [u for u in us if u[1] == q][-1]
                        pe.wait_ge(evac[q], last_u[0] + 1)

                    def scores(it):
                        h, n = ITS[it]
                        r = rows_of(h)
                        for g in (1, 2, 0):
                            w = widths(n)[g]
                            k0 = 128 * (n + 1) - w
                            if g == 0 and it >= 2:
                                pe.wait_ge(sem("pv_evac"), 8 * hp + it - 1)
                            last = nc.tensor.matmul(ps[:, SBANK[it % 2][g], 0:w], QKV[r, g, 0, 128 * n:128 * n + 128],
                                                    QKV[r, g, 1, k0:k0 + w], start=True, stop=True)
                        last.then_inc(sem("s_scores"), 1)

                    bat = 0
                    scores(0)
                    for it, (h, n) in enumerate(ITS):
                        if it + 1 < len(ITS):
                            scores(it + 1)
                        if bat >= 1:
                            pe.wait_ge(sem("pt_evac"), PER * hp + bat)
                        keep_warm(TBANK[bat % 2], WARM)
                        pe.wait_ge(sem("p_scaled"), 8 * hp + it + 1)
                        c = 0
                        groups = batches(key_tiles(n))
                        first = bat
                        for tiles in groups:
                            pe.wait_ge(sem("pt_evac"), PER * hp + bat - 1) if bat >= 2 else None
                            for i, _ in enumerate(tiles):
                                last = nc.tensor.transpose(ps[:, TBANK[bat % 2], 128 * i:128 * i + 128], SB[it % 2][:, c:c + 128], K("ident"))
                                c += 128
                            last.then_inc(sem("pt_done"), 1)
                            bat += 1
                        o = ps[rows_of(h), SBANK[it % 2][0], 256:384]
                        kt = 0
                        for i, tiles in enumerate(groups):
                            pe.wait_ge(sem("pt_evac"), PER * hp + first + i + 1)
                            for g, k in tiles:
                                last = nc.tensor.matmul(o, VT[:, g, k, 64 * h:64 * h + 64], PT[:, kt, :], start=(kt == 0),
                                                        stop=(kt == len(key_tiles(n)) - 1))
                                kt += 1
                        last.then_inc(sem("pv_done"), 1)
                    pe.wait_ge(sem("pv_evac"), 8 * hp + 8)
                    pe.wait_ge(sem("q_spread"), hp + 1)
                    for g in range(3):
                        nc.tensor.matmul(ps[:, 1, 128 + 64 * g:192 + 64 * g], QA[:, g, :], QKV[:, g, 1, SEQ:NT], start=(g == 0),
                                         stop=False, skip_group_check=True)
                    for b in range(DB):
                        pe.wait_ge(sem("kc_loaded%d" % (b % 2)), 16 * (4 * hp + b // 2 + 1))
                        o, k0 = slice(32 * (b // 2), 32 * (b // 2) + 32), 0
                        for g in range(3):
                            last = nc.tensor.matmul(ps[o, 1 + g, 0:CK[g]], QB[:, g, b, :], KC[b % 2][:, k0:k0 + CK[g]],
                                                    start=(g > 0 and b % 2 == 0), stop=(b % 2 == 1), skip_group_check=True)
                            k0 += CK[g]
                        last.then_inc(sem("kc_used"), 1)
                    pe.wait_ge(sem("sp_ready"), hp + 1)
                    for tl in range(3):
                        pe.wait_ge(sem("pt_evac"), PER * hp + bat - 1)
                        for i in range(4):
                            c, w = STILES[4 * tl + i]
                            last = nc.tensor.transpose(ps[0:w, TBANK[bat % 2], 128 * i:128 * i + 128], SB[0][:, c:c + w], K("ident"))
                        last.then_inc(sem("pt_done"), 1)
                        bat += 1
                    assert bat == PER
                    pe.wait_ge(sem("pt_evac"), PER * hp + PER)
                    for b in range(DB):
                        pe.wait_ge(sem("vc_loaded%d" % (b % 2)), 16 * (4 * hp + b // 2 + 1))
                        c = slice(16 * b, 16 * b + 16)
                        o = ps[32 * (b % 4):32 * (b % 4) + 16, 4, 128 * (b // 4):128 * (b // 4) + 128]
                        for k in range(9):
                            last = nc.tensor.matmul(o, PT[:, k, c], VC[b % 2][:, k, :], start=(k == 0), stop=False)
                        last.then_inc(sem("vc_used"), 1)
                        for g in range(3):
                            last = nc.tensor.matmul(o, PT[0:64, 9 + g, c], VS[:, g, :], start=False, stop=(g == 2))
                    last.then_inc(sem("so_done"), 1)
                    pe.wait_ge(sem("os_ready"), hp + 1)
                    for e in range(2):
                        last = nc.tensor.transpose(ps[:, 5, 128 * e:128 * e + 128], OS[:, 128 * e:128 * e + 128], K("ident"))
                    last.then_inc(sem("os_tr"), 1)

        def att_act(act, own):
            with act.Fori(0, 2) as cc:
                own.enter(cc, 2 * (2 * 6))
                for c2 in range(2):
                    hp = 2 * cc + c2

                    def guess(n):
                        act.wait_ge(sem("qk_norm"), 1 + 6 * hp + q_index(n) + 1)
                        act.wait_ge(sem("qk_applied"), 1 + 6 * hp + q_index(n))
                        rsqrt_act(own, bank2(4), arx[:, :], ary[:, :], 1.0 / DH, 0)

                    for P, q, n in at_units(cc, c2):
                        g, kind = QKV_ORDER[n]
                        act.wait_ge(unit_done, units_until(P, q))
                        if kind < 2:
                            act.wait_ge(sem("qk_norm"), 1 + 6 * hp + q_index(n))
                            nc.scalar.activation(two(asq[:, :]), bank2(2 * q), ACT.Square).then_inc(sem("qk_sq"), 1)
                            act.drain()
                        nc.scalar.activation(two(QKV[:, g, kind, :]), bank2(2 * q), ACT.Copy).then_inc(evac[q], 1)
                        act.drain()
                        split_hi(act, P + 1, q, W8)
                        if n and QKV_ORDER[n - 1][1] < 2:
                            guess(n - 1)
                    act.wait_ge(sem("qk_applied"), 1 + 6 * hp + 6)
                    act.wait_ge(evac[us_last(cc, c2)[1]], us_last(cc, c2)[0] + 1)
                    act.dma_start(t["kvT"][hp], QKV[:, :, 1:3, :]).then_inc(sem("kv_stored"), 16)
                    bat = 0
                    for it, (h, n) in enumerate(ITS):
                        w = sum(widths(n))
                        act.wait_ge(sem("p_max"), 9 * hp + it + 1)
                        nc.scalar.activation(SB[it % 2][:, 0:w], SB[it % 2][:, 0:w], ACT.Exp, bias=mx[:, it % 2],
                                             accum_out=ls[:, it % 2]).then_inc(sem("p_exp"), 1)
                        act.drain()
                        c = 0
                        for tiles in batches(key_tiles(n)):
                            act.wait_ge(sem("pt_done"), PER * hp + bat + 1)
                            m = len(tiles)
                            nc.scalar.activation(PT[:, c:c + m, :].rearrange("p k n -> p (k n)"), ps[:, TBANK[bat % 2], 0:128 * m],
                                                 ACT.Copy).then_inc(sem("pt_evac"), 1)
                            act.drain()
                            c += m
                            bat += 1
                    act.wait_ge(sem("p_max"), 9 * hp + 9)
                    nc.scalar.activation(SB[0][:, :], SB[0][:, :], ACT.Exp, bias=mx[:, 0], accum_out=ls[:, 0]).then_inc(sem("p_exp"), 1)
                    act.drain()
                    for tl in range(3):
                        act.wait_ge(sem("pt_done"), PER * hp + bat + 1)
                        full = 4 if tl < 2 else 1
                        b = TBANK[bat % 2]
                        ins = nc.scalar.activation(PT[:, 4 * tl:4 * tl + full, :].rearrange("p k n -> p (k n)"), ps[:, b, 0:128 * full], ACT.Copy)
                        if full == 1:
                            ins = nc.scalar.activation(PT[0:64, 9:12, :].rearrange("p k n -> p (k n)"), ps[0:64, b, 128:512], ACT.Copy)
                        ins.then_inc(sem("pt_evac"), 1)
                        act.drain()
                        bat += 1
                    act.wait_ge(sem("kv_stored"), 16 * (hp + 1))
                own.leave(2)

        def us_last(cc, c2):
            return at_units(cc, c2)[-1]

        def att_dve(dve, own):
            V = nc.vector
            V.memset(QB[:, :, :, :].rearrange("p g b n -> p (g b n)"), 0.0)
            V.memset(OS[:, :], 0.0)
            own(V.memset(QA[:, :, :].rearrange("p g n -> p (g n)"), 0.0))
            own(V.tensor_scalar(par[:, COLS["qg"]:COLS["qg"] + 3, 0], par[:, COLS["qg"]:COLS["qg"] + 3, 0], DH ** -0.5, None, ALU.mult))
            dve.wait_ge(sem("mask_loaded"), 16)
            with dve.Fori(0, 2) as cc:
                own.enter(cc, 2 * (3 * 6 + 2 * 9 + 8 + 1))
                for c2 in range(2):
                    hp = 2 * cc + c2
                    us = at_units(cc, c2)

                    def apply(n):
                        g, kind = QKV_ORDER[n]
                        rsqrt_dve(own, dve, RS_ATT + 6 * hp + q_index(n) + 1, arx[:, :], ary[:, :], art[:, :])
                        a = QKV[:, g, kind, :]
                        V.scalar_tensor_tensor(a, a, P1("qg" if kind == 0 else "kg", g), ary[:, :], ALU.mult, ALU.mult)\
                            .then_inc(sem("qk_applied"), 1)
                        dve.drain()

                    def v_out(g):
                        dve.wait_ge(sem("v_tr"), 3 * hp + g + 1)
                        V.tensor_copy(VT[:, g].rearrange("p t n -> p (t n)"), ps[:, 6, :])
                        V.tensor_copy(VS[:, g, :], ps[0:64, 7, 0:128]).then_inc(sem("v_evac"), 1)
                        dve.drain()

                    for n in range(9):
                        if QKV_ORDER[n][1] < 2:
                            apply(n)
                        else:
                            v_out(QKV_ORDER[n][0])
                    dve.wait_ge(sem("qk_applied"), 1 + 6 * hp + 6)
                    for h in range(2):
                        r = rows_of(h)
                        for g in range(3):
                            src = QKV[r, g, 0, SEQ:NT].rearrange("p (b t) -> p b t", t=DS)
                            for e in range(2):
                                V.tensor_copy(QB[r, g, e:DB:2, 16 * e + 8 * h:16 * e + 8 * h + 8], src[:, e:DB:2, :])
                            ins = V.tensor_copy(QA[r, g, :].rearrange("p (b n) -> p b n", n=16)[:, :, 8 * h:8 * h + 8], src)
                    ins.then_inc(sem("q_spread"), 1)
                    dve.drain()

                    def row_max(i, w):
                        own(V.reduce_max(mx[:, i], SB[i][:, 0:w], AX.X))
                        V.tensor_scalar(mx[:, i], mx[:, i], -1.0, None, ALU.mult).then_inc(sem("p_max"), 1)
                        dve.drain()

                    def biased(it):
                        h, n = ITS[it]
                        dve.wait_ge(sem("s_scores"), 8 * hp + it + 1)
                        if it >= 2:
                            dve.wait_ge(sem("pv_done"), 8 * hp + it - 1)
                        c = 0
                        for g, w in enumerate(widths(n)):
                            m0 = (256, 768, 1280)[g] - w
                            ins = V.scalar_tensor_tensor(SB[it % 2][:, c:c + w], MSK[:, m0:m0 + w], P1("slp", 2 * hp + h),
                                                         ps[:, SBANK[it % 2][g], 0:w], ALU.mult, ALU.add)
                            c += w
                        own(ins)
                        row_max(it % 2, c)

                    biased(0)
                    for it, (h, n) in enumerate(ITS):
                        w = sum(widths(n))
                        dve.wait_ge(sem("p_exp"), 9 * hp + it + 1)
                        own(V.reciprocal(ls[:, it % 2], ls[:, it % 2]))
                        V.tensor_scalar(SB[it % 2][:, 0:w], SB[it % 2][:, 0:w], ls[:, it % 2], None, ALU.mult).then_inc(sem("p_scaled"), 1)
                        if it + 1 < len(ITS):
                            biased(it + 1)
                        dve.wait_ge(sem("pv_done"), 8 * hp + it + 1)
                        V.tensor_copy(o_at[rows_of(h), hp, 128 * n:128 * n + 128], ps[rows_of(h), SBANK[it % 2][0], 256:384])\
                            .then_inc(sem("pv_evac"), 1)
                        dve.drain()
                    dve.wait_ge(sem("kc_used"), 1 + 8 * hp + 8)
                    for i, (c, w) in enumerate(((0, 320), (320, 512), (832, 512))):
                        ins = V.scalar_tensor_tensor(SB[0][:, c:c + w], MSK[:, 1280 + c:1280 + c + w], P1("sls", hp), ps[:, 1 + i, 0:w],
                                                     ALU.mult, ALU.add)
                    own(ins)
                    row_max(0, NKEY)
                    dve.wait_ge(sem("p_exp"), 9 * hp + 9)
                    own(V.reciprocal(ls[:, 0], ls[:, 0]))
                    V.tensor_scalar(SB[0][:, :], SB[0][:, :], ls[:, 0], None, ALU.mult).then_inc(sem("sp_ready"), 1)
                    dve.drain()
                    dve.wait_ge(sem("so_done"), hp + 1)
                    for e in range(4):
                        r = slice(32 * e, 32 * e + 16)
                        ins = V.tensor_copy(OS[r, :], ps[r, 4, 0:256])
                    ins.then_inc(sem("os_ready"), 1)
                    dve.wait_ge(sem("os_tr"), hp + 1)
                    for h in range(2):
                        r = rows_of(h)
                        ins = V.tensor_copy(o_at[r, hp, SEQ:NT].rearrange("p (b t) -> p b t", t=DS),
                                            ps[r, 5, 0:256].rearrange("p (b n) -> p b n", n=32)[:, :, 8 * h:8 * h + 8])
                    ins.then_inc(sem("so_evac"), 1)
                    dve.drain()
                own.leave(2)

        def merge_pe(pe):
            with pe.Fori(0, 4) as jj:
                for q in range(2):
                    unit_wait(pe, P_MRG + jj, q)
                    three_pass(q, o_hi, o_lo, 0, 4, 4 * q, ("o_split", 0, 0))
                    three_pass(q, o_hi[:, 4:8], o_lo[:, 4:8], 4, 4, 4 * q + 2, ("o_split", 4, 0)).then_inc(unit_done, 1)
            pe.wait_ge(sem("m_ready"), KD)
            units_and_squares(pe, 2, P_OUT, lambda P, q: unit(pe, P, q, m_hi, m_lo, ready=("m_ready", 1, KD - 1)))

        def merge_act(act):
            for k in range(8):
                src = o_at[:, k, :] if k < 4 else o_rw[:, k - 4, :]
                nc.scalar.activation(o_hi[:, k, :], src, ACT.Copy).then_inc(sem("o_hi_ready"), 1)
                act.drain()
            with act.Fori(0, 4) as jj:
                for q in range(2):
                    j = 2 * jj + q
                    act.wait_ge(sem("gates_in%d" % q), 16 * (jj + 1))
                    act.wait_ge(sem("mrg_ready"), 1 + j)
                    nc.scalar.activation(sA[:, :], GI[q][:, 0, :], ACT.Sigmoid)
                    nc.scalar.activation(sR[:, :], GI[q][:, 1, :], ACT.Sigmoid).then_inc(sem("sig_ready"), 1)
                    split_hi(act, P_MRG + jj + 1, q, W8)
                    act.wait_ge(sem("mrg_ready"), 1 + j + 1)
                    nc.scalar.activation(m_hi[:, j, :], mA[:, :], ACT.Copy).then_inc(sem("m_hi_ready"), 1)
                    act.drain()
            splits_and_squares(act, 2, P_OUT, W8)

        def merge_dve(dve, own):
            V = nc.vector
            for k in range(8):
                src = o_at[:, k, :] if k < 4 else o_rw[:, k - 4, :]
                dve.wait_ge(sem("o_hi_ready"), k + 1)
                V.tensor_tensor(o_lo[:, k, :], src, o_hi[:, k, :].bitcast(F32), ALU.subtract).then_inc(sem("o_split"), 1)
                dve.drain()
            with dve.Fori(0, 4) as jj:
                own.enter(jj, 2)
                for q in range(2):
                    j = 2 * jj + q
                    P = P_MRG + jj
                    dve.wait_ge(sem("sig_ready"), j + 1)
                    dve.wait_ge(unit_done, units_until(P, q))
                    own(V.tensor_tensor(two(mA[:, :]), two(sA[:, :]), bank2(4 * q), ALU.mult))
                    V.tensor_tensor(two(sR[:, :]), two(sR[:, :]), bank2(4 * q + 2), ALU.mult).then_inc(evac[q], 1)
                    dve.drain()
                    dve.wait_ge(evac[q], P + 1)
                    V.tensor_tensor(mA[:, :], mA[:, :], sR[:, :], ALU.add).then_inc(sem("mrg_ready"), 1)
                    dve.drain()
                    dve.wait_ge(sem("mrg_ready"), 1 + j + 1)
                    dve.wait_ge(sem("m_hi_ready"), j + 1)
                    V.tensor_tensor(m_lo[:, j, :], mA[:, :], m_hi[:, j, :].bitcast(F32), ALU.subtract).then_inc(sem("m_ready"), 1)
                    dve.drain()
                own.leave(4)
            with dve.Fori(0, 4) as jj:
                for q in range(2):
                    P = P_OUT + jj
                    dve.wait_ge(unit_done, 2 * P + q + 1)
                    V.tensor_tensor(two(x[:, 2 * jj + q, :]), two(x[:, 2 * jj + q, :]), bank2(2 * q), ALU.add).then_inc(evac[q], 1)
                    dve.drain()

        block = ctx.enter_context(nc.Block())
        own_act, own_dve = sem("act_own_steps"), sem("dve_own_steps")

        from_one = {"pe": ("kc_used", "vc_used", "lora_done", "qk_norm"),
                    "act": ("o_evac",),
                    "dve": ("v_evac", "so_evac", "qk_applied", "m_ready", "mrg_ready")}

        def begin(eng, which):
            for name in from_one[which]:
                eng.drain().then_inc(sem(name), 1)

        @block.tensor
        def _(pe):
            begin(pe, "pe")
            first_squares_pe(pe)
            ffn_pe(pe, 0, P_FFN1)
            barrier(pe, 1)
            rwkv_pe(pe)
            barrier(pe, 2)
            rwsam_pe(pe)
            rwout_pe(pe)
            barrier(pe, 3)
            att_pe(pe)
            barrier(pe, 4)
            merge_pe(pe)
            barrier(pe, 5)
            ffn_pe(pe, 1, P_FFN2)
            barrier(pe, 6)

        @block.scalar
        def _(act):
            begin(act, "act")
            own = Own(act, own_act)
            for i in range(XL):
                act.dma_start(x[:, 2 * i:2 * i + 2, :], t["xT"][:, 2 * i:2 * i + 2, :]).then_inc(sem("x_loaded%d" % i), 16)
                if i == 0:
                    act.dma_start(con[:, 0:CFIRST], t["con"][:, 0:CFIRST]).then_inc(sem("con_loaded"), 16)
                    act.dma_start(par[:, :, 0], t["par"]).then_inc(sem("con_loaded"), 16)
            act.dma_start(con[:, CFIRST:NCONST], t["con"][:, CFIRST:NCONST]).then_inc(sem("masks_loaded"), 16)
            first_squares_act(act)
            norm_act(act, own, 0)
            for q in range(2):
                split_hi(act, 0, q, W8)
            ffn_act(act, 0, P_FFN1)
            barrier(act, 1)
            norm_act(act, own, 1)
            rwkv_act(act, own)
            barrier(act, 2)
            rwsam_act(act, own)
            rwout_act(act, own)
            act.wait_ge(sem("wkvp_stored"), 16 * CT)
            act.wait_ge(sem("wkvs_stored"), 16 * CT)
            act.wait_ge(sem("shift_stored"), 16)
            barrier(act, 3)
            att_act(act, own)
            barrier(act, 4)
            merge_act(act)
            barrier(act, 5)
            norm_act(act, own, 2)
            ffn_act(act, 1, P_FFN2)
            barrier(act, 6)

        @block.vector
        def _(dve):
            begin(dve, "dve")
            own = Own(dve, own_dve)
            norm_dve(dve, own, 0, "g1")
            ffn_dve(dve, 0, P_FFN1)
            barrier(dve, 1)
            norm_dve(dve, own, 1, "gm")
            rwkv_dve(dve, own)
            barrier(dve, 2)
            rwsam_dve(dve, own)
            rwout_dve(dve, own)
            barrier(dve, 3)
            att_dve(dve, own)
            barrier(dve, 4)
            merge_dve(dve, own)
            barrier(dve, 5)
            norm_dve(dve, own, 2, "g2")
            ffn_dve(dve, 1, P_FFN2)
            barrier(dve, 6)

        @block.gpsimd
        def _(pool):
            ffn_pool(pool, P_FFN1)
            with pool.Fori(P_RW, P_FFN2) as P:
                for q in range(2):
                    split_lo(pool, P, q, W8)
            ffn_pool(pool, P_FFN2)

        @block.sync
        def _(sp):
            ffn_sp(sp, P_FFN1, 0, 0)

            def mid_pair(P):
                for q in range(2):
                    load_unit(sp, P, q, t["w8"][44 + 2 * (P - P_RW) + q], W8)

            def gates(j):
                return t["gates"][bass.ds(2 * j, 2)].rearrange("g p n -> p g n")

            mid_pair(P_RW)
            mid_pair(P_RW + 1)
            sp.wait_ge(sem("h_ready"), 16)
            sp.dma_start(SH0[:, :, :], t["shift0"]).then_inc(sem("rw_loaded"), 16)
            sp.dma_start(GL[:, :], t["g_up"]).then_inc(sem("rw_loaded"), 16)
            with sp.Fori(0, 2) as cc:
                sp.wait_ge(sem("lora_done"), 1 + 4 * cc)
                for c2 in range(2):
                    sp.dma_start(LO[c2][:, :], t["lora"][2 * cc + c2]).then_inc(sem("lora_w%d" % c2), 16)
                for i in range(7):
                    mid_pair(P_RW + 2 + 7 * cc + i)
                    copy_cache(sp, 2, 49 + 7 * cc + i)
            mid_pair(P_ATT + 1)
            copy_cache(sp, 2, 63)
            sp.wait_ge(sem("phase2_over"), 3)
            sp.dma_start(SST, t["state"]).then_inc(sem("s_states"), 16)
            sp.wait_ge(sem("phase3_over"), 3)
            sp.dma_start(MSK[:, :], t["masks"]).then_inc(sem("mask_loaded"), 16)
            with sp.Fori(0, 2) as cc:
                for c2 in range(2):
                    hp = 2 * cc + c2
                    for i in range(9):
                        k = 9 * c2 + i
                        load_unit(sp, P_ATT + 2 + 9 * cc + k // 2, k % 2, t["w8"][44 + 2 * (P_ATT + 2 - P_RW) + 18 * cc + k], W8)
                        if i % 2 == 0:
                            copy_cache(sp, 1, 8 + 5 * hp + i // 2)

                    def k_load(b):
                        sp.wait_ge(sem("kc_used"), 1 + 8 * hp + b - 1) if b >= 2 else sp.wait_ge(sem("kc_used"), 1 + 8 * hp)
                        sp.dma_start(KC[b % 2][:, :], t["kc"][hp, b]).then_inc(sem("kc_loaded%d" % (b % 2)), 16)

                    def v_load(b):
                        sp.wait_ge(sem("vc_used"), 1 + 8 * hp + b - 1) if b >= 2 else sp.wait_ge(sem("vc_used"), 1 + 8 * hp)
                        sp.dma_start(VC[b % 2][:, :, :], t["vc"][hp, b]).then_inc(sem("vc_loaded%d" % (b % 2)), 16)

                    for b in range(2):
                        k_load(b)
                        v_load(b)
                    for b in range(2, DB):
                        k_load(b)
                    for b in range(2, DB):
                        v_load(b)
            sp.wait_ge(sem("phase4_over"), 3)
            for q in range(2):
                sp.wait_ge(sem("gate_stored%d" % q), 16 * 2 * CT)
                sp.dma_start(GI[q][:, :, :], gates(q)).then_inc(sem("gates_in%d" % q), 16)
            with sp.Fori(P_MRG + 2, P_FFN2 - 3) as P:
                for q in range(2):
                    load_unit(sp, P, q, t["w8"][44 + 2 * (P - P_RW) + q], W8)
                    sp.wait_ge(sem("sig_ready"), 2 * (P - P_MRG - 2) + q + 1)
                    sp.dma_start(GI[q][:, :, :], gates(2 * (P - P_MRG - 1) + q)).then_inc(sem("gates_in%d" % q), 16)
                copy_cache(sp, 2, P - (P_MRG + 2) + 43)
            with sp.Fori(P_FFN2 - 3, P_FFN2) as P:
                mid_pair(P)
                copy_cache(sp, 2, P - (P_MRG + 2) + 43)
            ffn_sp(sp, P_FFN2, 126, 16)
            for q in range(2):
                load_unit(sp, N_PAIR, q, t["w8"][170 + q], W8)
            sp.wait_ge(sem("phase6_over"), 3)
            sp.dma_start(t["yT"], x[:, :, :]).then_inc(sem("y_stored"), 16)
            sp.wait_ge(sem("y_stored"), 16)
            sp.wait_ge(sem("cache_copied"), 16 * N_PIECE)
            sp.wait_ge(sem("kv_stored"), 16 * CT)
            sp.wait_ge(sem("wkvp_stored"), 16 * CT)
            sp.wait_ge(sem("wkvs_stored"), 16 * CT)
            sp.wait_ge(sem("shift_stored"), 16)


def tiles8(w, cols):
    k = w.shape[0] // 128
    return w[:, cols:cols + 128].reshape(k, 128, 128).transpose(1, 0, 2).reshape(128, k * 128)


def kernel(**inputs):
    import concourse.bacc as bacc
    from concourse.bass_utils import run_bass_kernel_spmd

    a = {k: np.asarray(v) for k, v in inputs.items()}
    f32 = np.float32
    A_COLS, S_COLS = 3 * 3 * 512, 1792
    w_in = a["w_in"][0]
    zero = np.zeros((128, W8), f32)

    def ffn8(f):
        g, u = a["ffn%d_w_gate" % f][0], a["ffn%d_w_up" % f][0]
        return [tiles8(m, 128 * j) for j in range(NF) for m in (g, u)]

    def ffn11(f):
        d = a["ffn%d_w_down" % f][0]
        return [tiles8(d[HALF * 128 * hf:HALF * 128 * (hf + 1)], 128 * j) for hf in range(2) for j in range(KD)]

    mids = [tiles8(w_in, A_COLS + 128 * i) for i in (12, 13)]
    for ct in range(CT):
        mids += [tiles8(w_in, A_COLS + 128 * (4 * n + ct)) for n in range(3)]
        mids += [tiles8(w_in, A_COLS + S_COLS + D * branch + 128 * (2 * ct + i)) for i in range(2) for branch in range(2)]
    mids += [tiles8(w_in, 1536 * g + 512 * kind + 128 * hp) for hp in range(CT) for g, kind in QKV_ORDER]
    wa, wr, wo = a["w_branch_attn"][0], a["w_branch_rwkv"][0], a["w_out"][0]
    for j in range(KD):
        mids.append(np.concatenate([tiles8(wa, 128 * j), tiles8(wr, 128 * j)], axis=1))
    mids += [tiles8(wo, 128 * j) for j in range(KD)]
    w8 = np.stack(ffn8(1) + mids + ffn8(2) + [zero, zero])
    w11 = np.stack(ffn11(1) + ffn11(2))

    def cols(v, n):
        return v.reshape(n, 128).T

    slopes = (2.0 ** (-np.arange(1, 9, dtype=np.float64))).astype(f32)
    par = np.concatenate([
        cols(a["ffn1_norm"][0], 8), cols(a["mix_norm"][0], 8), cols(a["ffn2_norm"][0], 8), cols(a["rwkv_mu"][0], 14),
        cols(a["rwkv_w0"][0], 4), cols(a["rwkv_a0"][0], 4), cols(a["rwkv_k_k"][0], 4), cols(a["rwkv_k_a"][0], 4),
        cols(a["rwkv_r_k"][0].reshape(-1), 4), cols(a["rwkv_ln_gain"][0], 4), cols(a["rwkv_ln_bias"][0], 4),
        np.concatenate([a["attn_q_norm"][0]] * 2, axis=1).T, np.concatenate([a["attn_k_norm"][0]] * 2, axis=1).T,
        np.broadcast_to(slopes, (128, 8)),
        slopes.reshape(4, 2)[:, (np.arange(128) // 8) % 2].T,
        np.broadcast_to(np.array([RMS_EPS, KK_EPS, LN_EPS], f32), (128, 3))], axis=1)
    con, masks = constants()
    xs = np.concatenate([a["x_prompt"][0], a["x_sample"].reshape(NS, D)])
    caches = [a["cache_kv_w%d" % w][0] for w, _ in GROUPS]
    kcs, vcs = [], []
    for g in range(3):
        c = caches[g][:, sample_positions(g)]
        kcs.append(c[:, :, 0].reshape(DB, CK[g], CT, 128).transpose(2, 0, 3, 1))
        vcs.append(c[:, :, 1].reshape(DB, CK[g] // 128, 128, CT, 128).transpose(3, 0, 2, 1, 4))
    arrays = {
        "xT": xs.T.reshape(KD, 128, NT).transpose(1, 0, 2), "par": par, "con": con, "masks": masks, "w8": w8, "w11": w11,
        "shift0": a["state_shift"][0].T.reshape(SHT, 128, DB).transpose(1, 0, 2), "g_up": a["rwkv_g_lora_up"][0],
        "lora": np.concatenate([a["rwkv_w_lora_up"][0], a["rwkv_a_lora_up"][0]]).reshape(128, CT, 128).transpose(1, 0, 2),
        "state": a["state_wkv"][0].reshape(DB, CT, 2, DH, DH).transpose(2, 4, 1, 0, 3).reshape(128, CT, 512),
        "kc": np.concatenate(kcs, axis=3), "vc": np.concatenate(vcs, axis=3),
    }
    for g in range(3):
        arrays["cache%d" % g] = caches[g].reshape(DB, PASTS[g], 1024)
    arrays = {k: np.ascontiguousarray(v, dtype=f32) for k, v in arrays.items()}
    outs = {"yT": (128, KD, NT), "kvT": (CT, 128, 3, 2, NT), "wkv_p": (CT, 128, DH), "wkv_s": (CT, 128, 512), "shift": (128, SHT, 9),
            "gates": (2 * KD, 128, NT)}
    for g in range(3):
        outs["cache_out%d" % g] = (DB, PASTS[g] - (DS if g < 2 else 0), 1024)
    nc = bacc.Bacc("TRN2", target_bir_lowering=False, num_devices=1)
    t = {k: nc.dram_tensor("in_" + k, v.shape, F32, kind="ExternalInput").ap() for k, v in arrays.items()}
    t.update({k: nc.dram_tensor(k, s, F32, kind="ExternalOutput").ap() for k, s in outs.items()})
    build(nc, t)
    r = run_bass_kernel_spmd(nc, [{"in_" + k: v for k, v in arrays.items()}], core_ids=[0]).results[0]

    y = r["yT"].transpose(2, 1, 0).reshape(NT, D)
    kv = r["kvT"].reshape(CT, 2, DH, 3, 2, NT).transpose(3, 5, 4, 0, 1, 2).reshape(3, NT, 2, 8, DH)
    kv_p = [kv[g, max(0, SEQ - GROUPS[g][0]):SEQ][None, None] for g in range(3)]
    kv_s = [np.concatenate([r["cache_out%d" % g].reshape(DB, -1, 2, 8, DH), kv[g, SEQ:].reshape(DB, DS, 2, 8, DH)], axis=1)[None]
            for g in range(3)]
    wkv_p = r["wkv_p"].reshape(CT, 2, DH, DH).transpose(0, 1, 3, 2).reshape(1, 1, 8, DH, DH)
    wkv_s = r["wkv_s"].reshape(CT, 2, DH, DB, DH).transpose(3, 0, 1, 4, 2).reshape(1, DB, 8, DH, DH)
    sh = r["shift"].transpose(2, 1, 0).reshape(9, SHT * 128)
    return (y[:SEQ][None], y[SEQ:].reshape(DB, DS, D), *kv_p, wkv_p, sh[None, :1], *kv_s, wkv_s, sh[None, 1:])
```
